# Optimizing a Trainium2 kernel written in Bass

```python
import jax, jax.numpy as jnp
from jax import lax
import numpy as np

D_MODEL = 1024
BATCH = 1
SEQ = 512
DEPTH = 2

CHUNK = 64
N_MIXERS = 2
N_HEADS = 16
HEAD_DIM = D_MODEL // N_HEADS
D_FF = 4 * D_MODEL
CONV_WIDTH = 31
Q_BLOCK = 128
RMS_EPS = 1e-6
LN_EPS = 1e-5
MASK_VALUE = -1e30
N_CONV_LAYERS = (DEPTH + 1) // 2
N_ATTN_LAYERS = DEPTH // 2

kernel_name = "hybrid_conformer_conv_fox_sqrelu_sandwich"

def rmsnorm(x, g):
    xf = x.astype(jnp.float32)
    y = xf * lax.rsqrt(jnp.mean(jnp.square(xf), axis=-1, keepdims=True) + RMS_EPS)
    return (y * g.astype(jnp.float32)).astype(x.dtype)

def layernorm(x, g, b):
    xf = x.astype(jnp.float32)
    mu = jnp.mean(xf, axis=-1, keepdims=True)
    var = jnp.mean(jnp.square(xf - mu), axis=-1, keepdims=True)
    y = (xf - mu) * lax.rsqrt(var + LN_EPS)
    return (y * g.astype(jnp.float32) + b.astype(jnp.float32)).astype(x.dtype)

def conformer_conv(h, pw1_w, pw1_b, dw_w, dw_b, ln_g, ln_b, pw2_w, pw2_b):
    a = h @ pw1_w + pw1_b
    u, gate = jnp.split(a, 2, axis=-1)
    u = u * jax.nn.sigmoid(gate)
    y = lax.conv_general_dilated(
        u, dw_w[:, None, :],
        window_strides=(1,),
        padding=((CONV_WIDTH - 1, 0),),
        dimension_numbers=("NWC", "WIO", "NWC"),
        feature_group_count=D_MODEL) + dw_b
    y = layernorm(y, ln_g, ln_b)
    y = jax.nn.silu(y)
    return y @ pw2_w + pw2_b

def forgetting_attention(h, w_in, b_f, w_o):
    B, S, _ = h.shape
    proj = h @ w_in
    q = proj[..., :D_MODEL]
    k = proj[..., D_MODEL:2 * D_MODEL]
    v = proj[..., 2 * D_MODEL:3 * D_MODEL]
    f_logit = proj[..., 3 * D_MODEL:].astype(jnp.float32) + b_f.astype(jnp.float32)
    log_f = jax.nn.log_sigmoid(f_logit)
    F = jnp.cumsum(log_f, axis=1).transpose(0, 2, 1)

    def heads(t):
        return t.reshape(B, S, N_HEADS, HEAD_DIM).transpose(0, 2, 1, 3)
    q, k, v = heads(q), heads(k), heads(v)

    n_blocks = S // Q_BLOCK
    qb = q.reshape(B, N_HEADS, n_blocks, Q_BLOCK, HEAD_DIM).transpose(2, 0, 1, 3, 4)
    Fq = F.reshape(B, N_HEADS, n_blocks, Q_BLOCK).transpose(2, 0, 1, 3)
    kpos = jnp.arange(S)
    scale = HEAD_DIM ** -0.5

    def attend(args):
        q_blk, f_blk, blk = args
        qpos = blk * Q_BLOCK + jnp.arange(Q_BLOCK)
        s = jnp.einsum("bhqd,bhkd->bhqk", q_blk, k,
                       preferred_element_type=jnp.float32) * scale
        s = s + (f_blk[..., None] - F[:, :, None, :])
        s = jnp.where(kpos[None, :] <= qpos[:, None], s, MASK_VALUE)
        p = jax.nn.softmax(s, axis=-1)
        return jnp.einsum("bhqk,bhkd->bhqd", p.astype(v.dtype), v)

    o = lax.map(attend, (qb, Fq, jnp.arange(n_blocks)))
    o = o.transpose(1, 0, 3, 2, 4).reshape(B, S, D_MODEL)
    return o @ w_o

def sqrelu_mlp(h, w_up, w_down):
    return jnp.square(jax.nn.relu(h @ w_up)) @ w_down

def setup_inputs(seed: int = 0) -> dict:
    key = jax.random.key(seed)
    ks = jax.random.split(key, 20)
    f32 = jnp.float32
    D, H = D_MODEL, N_HEADS
    nrm = lambda k, shape, s: jax.random.normal(k, shape, f32) * s
    return {
        "x": jax.random.normal(ks[0], (BATCH, SEQ, D), f32),
        "g_mix_pre": 1.0 + nrm(ks[1], (DEPTH, D), 0.02),
        "g_mix_post": 1.0 + nrm(ks[2], (DEPTH, D), 0.02),
        "g_ffn_pre": 1.0 + nrm(ks[3], (DEPTH, D), 0.02),
        "g_ffn_post": 1.0 + nrm(ks[4], (DEPTH, D), 0.02),
        "conv_pw1_w": nrm(ks[5], (N_CONV_LAYERS, D, 2 * D), D ** -0.5),
        "conv_pw1_b": nrm(ks[6], (N_CONV_LAYERS, 2 * D), 0.02),
        "conv_dw_w": nrm(ks[7], (N_CONV_LAYERS, CONV_WIDTH, D), CONV_WIDTH ** -0.5),
        "conv_dw_b": nrm(ks[8], (N_CONV_LAYERS, D), 0.02),
        "conv_ln_g": 1.0 + nrm(ks[9], (N_CONV_LAYERS, D), 0.02),
        "conv_ln_b": nrm(ks[10], (N_CONV_LAYERS, D), 0.02),
        "conv_pw2_w": nrm(ks[11], (N_CONV_LAYERS, D, D), D ** -0.5),
        "conv_pw2_b": nrm(ks[12], (N_CONV_LAYERS, D), 0.02),
        "attn_w_in": nrm(ks[13], (N_ATTN_LAYERS, D, 3 * D + H), D ** -0.5),
        "attn_b_f": 1.0 + nrm(ks[14], (N_ATTN_LAYERS, H), 0.5),
        "attn_w_o": nrm(ks[15], (N_ATTN_LAYERS, D, D), D ** -0.5),
        "mlp_w_up": nrm(ks[16], (DEPTH, D, D_FF), D ** -0.5),
        "mlp_w_down": nrm(ks[17], (DEPTH, D_FF, D), D_FF ** -0.5),
    }

def reference(x, g_mix_pre, g_mix_post, g_ffn_pre, g_ffn_post,
              conv_pw1_w, conv_pw1_b, conv_dw_w, conv_dw_b, conv_ln_g, conv_ln_b,
              conv_pw2_w, conv_pw2_b, attn_w_in, attn_b_f, attn_w_o,
              mlp_w_up, mlp_w_down):
    for i in range(DEPTH):
        j = i // N_MIXERS
        h = rmsnorm(x, g_mix_pre[i])
        if i % N_MIXERS == 0:
            m = conformer_conv(h, conv_pw1_w[j], conv_pw1_b[j], conv_dw_w[j], conv_dw_b[j],
                               conv_ln_g[j], conv_ln_b[j], conv_pw2_w[j], conv_pw2_b[j])
        else:
            m = forgetting_attention(h, attn_w_in[j], attn_b_f[j], attn_w_o[j])
        x = x + rmsnorm(m, g_mix_post[i])
        h = rmsnorm(x, g_ffn_pre[i])
        x = x + rmsnorm(sqrelu_mlp(h, mlp_w_up[i], mlp_w_down[i]), g_ffn_post[i])
    return x


_drawn_inputs = setup_inputs


def setup_inputs(seed=0):
    import zlib

    import numpy as np

    out = dict(_drawn_inputs(seed))
    spreads = {}
    factors = {'g_mix_post': 2.866,
     'g_ffn_pre': 3.336,
     'g_ffn_post': 10.733,
     'conv_pw1_b': 3.153,
     'conv_ln_g': 2.83,
     'conv_ln_b': 3.283,
     'conv_pw2_b': 4.759}
    for name, (base, spread) in spreads.items():
        noise = np.random.default_rng([zlib.crc32(name.encode()), seed]).standard_normal(out[name].shape)
        drawn = base * np.exp(spread * noise) if base else spread * noise
        out[name] = __import__('jax').numpy.asarray(drawn.astype(out[name].dtype))
    for name, factor in factors.items():
        out[name] = (out[name] * factor).astype(out[name].dtype)
    return out
```

```python
import concourse.bass as bass
from concourse import mybir

F32 = mybir.dt.float32
F32R = mybir.dt.float32r
ALU = mybir.AluOpType
ACT = mybir.ActivationFunctionType
ds = bass.ds

P = 128
D = 1024
S = 512
KB = D // P
TB = S // P
FF = 4 * D
HEADS = 16
HD = D // HEADS
PAIRS = HEADS // 2
W = 31
PADW = S + W + 1
PE_TAPS = 12
DVE_TAPS = W - PE_TAPS
MASK = 1e30
RMS_EPS = 1e-6
LN_EPS = 1e-5

N_PW1 = 0
N_PW2 = N_PW1 + 4
N_MLP0 = N_PW2 + 2
N_ATT = N_MLP0 + 16
N_WO = N_ATT + PAIRS
N_MLP1 = N_WO + 2
STEPS = N_MLP1 + 16

V_MIX_PRE, V_MIX_POST, V_FFN_PRE, V_FFN_POST = 0, 2, 4, 6
V_PW1B, V_DWB, V_LNG, V_LNB, V_PW2B, V_DW = 8, 10, 11, 12, 13, 14
V_ROWS = V_DW + W

ST_PRE0, ST_MEAN, ST_VAR = 0, 1, 2
ST_POST = (3, 5, 7, 9)
ST_PRE = (0, 4, 6, 8)

SEQ = [("S", 0), ("S", 1), ("V", 0), ("P", 0), ("S", 2), ("S", 3), ("P", 1), ("S", 4), ("S", 5),
       ("P", 2), ("S", 6), ("S", 7), ("P", 3), ("T", 0), ("P", 4), ("T", 1), ("P", 5), ("T", 2),
       ("P", 6), ("T", 3), ("P", 7), ("O", 0), ("T", 4), ("P", 8), ("T", 5), ("P", 9), ("T", 6),
       ("P", 10), ("T", 7), ("P", 11), ("O", 1)]


def build(nc, x, g_mix_pre, g_mix_post, g_ffn_pre, g_ffn_post, conv_pw1_w, conv_pw1_b, conv_dw_w,
          conv_dw_b, conv_ln_g, conv_ln_b, conv_pw2_w, conv_pw2_b, attn_w_in, attn_b_f, attn_w_o,
          mlp_w_up, mlp_w_down, out):
    at = [0]
    base = (nc.sbuf_base + 63) // 64 * 64
    nc.alloc_sbuf_tensor("slab", [P, (nc.sbuf_usable_end - nc.sbuf_base - 256) // 4], F32)

    def put(name, shape, dt, where=None):
        n = 4
        for s in shape[1:]:
            n *= s
        pos = at[0] if where is None else where[0]
        t = nc.alloc_sbuf_tensor_at(name, shape, dt, offset=base + pos)
        if where is None:
            at[0] += (n + 31) // 32 * 32
        else:
            where[0] += (n + 31) // 32 * 32
        return t

    xT = put("xT", [P, KB, S], F32)
    at_h = [at[0]]
    hhi = put("hhi", [P, KB, S], F32R)
    at_out = [at[0]]
    hlo = put("hlo", [P, KB, S], F32R)
    m_wo = put("m_wo", [P, KB, S], F32, at_h)
    outsb = put("outsb", [P, TB, D], F32, at_out)
    wraw = put("wraw", [P, 2, KB, 2 * P], F32)
    whi = put("whi", [P, 4, KB, P], F32R)
    wlo = put("wlo", [P, 4, KB, P], F32R)
    at_m, at_m2 = [at[0]], [at[0]]
    m = put("m", [P, KB, S], F32)
    xin = put("xin", [P, TB, D], F32, at_m)
    ohi = put("ohi", [P, KB, S], F32R, at_m2)
    olo = put("olo", [P, KB, S], F32R)
    arena = at[0]
    ahi = put("ahi", [P, 16, S], F32R)
    alo = put("alo", [P, 16, S], F32R)
    ca = [arena]
    y = put("y", [P, KB, S], F32, ca)
    upad = put("upad", [P, 2, PADW], F32, ca)
    uhi = put("uhi", [P, 2, PADW], F32R, ca)
    ulo = put("ulo", [P, 2, PADW], F32R, ca)
    acc1 = put("acc1", [P, S], F32, ca)
    dwhi = put("dwhi", [P, KB, PE_TAPS], F32R, ca)
    dwlo = put("dwlo", [P, KB, PE_TAPS], F32R, ca)
    cb = [ca[0]]
    diaghi = put("diaghi", [P, 2, PE_TAPS, P], F32R, ca)
    diaglo = put("diaglo", [P, 2, PE_TAPS, P], F32R, ca)
    vrows = put("vrows", [P, D], F32, cb)
    assert ca[0] <= at[0], (ca[0], at[0])
    aa = [arena]
    qhi = put("qhi", [P, S], F32R, aa)
    qlo = put("qlo", [P, S], F32R, aa)
    kzhi = put("kzhi", [P, 2, S], F32R, aa)
    kzlo = put("kzlo", [P, 2, S], F32R, aa)
    vhi = put("vhi", [P, TB, P], F32R, aa)
    vlo = put("vlo", [P, TB, P], F32R, aa)
    prob = put("prob", [P, 2, 10 * P], F32, aa)
    rhsF = put("rhsF", [P, S], F32R, aa)
    lhsB = put("lhsB", [P, S], F32, aa)
    lhsF = put("lhsF", [P, 2, S], F32R, aa)
    causal = put("causal", [P, S], F32, aa)
    ab, ac = [aa[0]], [aa[0]]
    pThi = put("pThi", [P, TB, S], F32R, aa)
    pTlo = put("pTlo", [P, TB, S], F32R, aa)
    wfhi = put("wfhi", [P, KB, P], F32R, ab)
    wflo = put("wflo", [P, KB, P], F32R, ab)
    Fhi = put("Fhi", [P, S], F32R, aa)
    fwork = put("fwork", [P, 7, S], F32, ac)
    FZ, FB, FABS, FEXP, FLN, FLOG, FCUM = range(7)
    assert aa[0] <= at[0], (aa[0], at[0])
    tmp = put("tmp", [P, 4, S], F32)
    sumsq = put("sumsq", [P, S], F32)
    rinv = put("rinv", [P, S], F32)
    vec = put("vec", [P, KB, V_ROWS], F32)
    ident = put("ident", [P, P], F32)
    ones = put("ones", [P, P], F32)
    wfraw = put("wfraw", [P, KB, HEADS], F32)
    onehot = put("onehot", [P, HEADS], F32)
    bf = put("bf", [P, 1], F32)
    eps = put("eps", [P, 2], F32)
    negmax = put("negmax", [P, 8], F32)
    den = put("den", [P, 8], F32)
    rden = put("rden", [P, 8], F32)
    assert base + at[0] <= nc.sbuf_usable_end - 256, (base + at[0], nc.sbuf_usable_end)

    psum = nc.alloc_psum_tensor("psum", [P, 8, 512], F32)
    STAT, SCORE, TRP, OUTP = 6, 4, 6, 7

    sem_names = (
        "x_loaded vec_loaded wf_loaded raw0 raw1 consts zeroed "
        "vt_done vec_ready xt_done xt_copied "
        "w_hi0 w_hi1 w_ready0 w_ready1 unit0 unit1 "
        "h_hi h_ready p_sq p_sum stat root rinv_done "
        "m_done m_sq m_sum m_zero t1_done x_done "
        "glu_t glu_g glu_s glu_u u_hi u_ready dw_hi dw_lo diag conv_done tap acc y_done y_sum y_zero "
        "c_sub c_sq c_sum c_nrm c_silu c_hi c_ready "
        "up_evac up_sq up_hi a_ready dn_evac "
        "wf_zero wf_hi wf_ready f_done f_z f_b f_abs f_exp f_ln f_log f_cum f_hi f_lo f_rows f_base f_ready sel "
        "pr_evac q_hi q_ready k_hi k_ready vtr v_hi v_ready "
        "sc_done sc_seen sc_evac ex_done rc_done p_ready t_done p_hi pt_ready pv_done o_hi o_ready "
        "out_tr out_copied stored"
    ).split()
    s = {n: nc.alloc_semaphore(n) for n in sem_names}
    raw = (s["raw0"], s["raw1"])
    w_hi = (s["w_hi0"], s["w_hi1"])
    w_ready = (s["w_ready0"], s["w_ready1"])
    unit = (s["unit0"], s["unit1"])

    def flat(ap):
        return ap.rearrange("p a b -> p (a b)")

    def vcol(row, k):
        if isinstance(k, int):
            return vec[:, k, row:row + 1]
        return flat(vec[:, ds(k, 1), row:row + 1])

    def blk(t, k):
        if isinstance(k, int):
            return t[:, k, :]
        return flat(t[:, ds(k, 1), :])

    def probs(hh, j):
        o = P * (j * (j + 1) // 2)
        return prob[:, hh, o:o + P * (j + 1)]

    def mbuf(b):
        return m_wo if b == 2 else m

    with nc.Block() as block:

        @block.sync
        def _(sp):
            def load(n, r, parts):
                if not (isinstance(n, int) and n == 0):
                    sp.wait_ge(w_ready[r], 2 * n)
                for dst, src in parts:
                    sp.dma_start(dst, src).then_inc(raw[r], 16)

            def by_rows(w, r, col):
                wr = w.rearrange("(k p) f -> p k f", p=P)
                c = col if isinstance(col, int) else None
                sl = slice(c, c + 2 * P) if c is not None else ds(col, 2 * P)
                return [(wraw[:, r, 4 * k:4 * k + 4, :], wr[:, 4 * k:4 * k + 4, sl]) for k in range(2)]

            def by_cols(w, r, cols):
                wr = w.rearrange("(k p) f -> p k f", p=P)
                return [(wraw[:, r, :, P * c:P * c + P], wr[:, :, ds(cols[c], P)]) for c in range(2)]

            for q in range(TB):
                sp.dma_start(xin[:, q, :], x[0, q * P:(q + 1) * P, :]).then_inc(s["x_loaded"], 16)
            rows = [(V_MIX_PRE, 2, g_mix_pre), (V_MIX_POST, 2, g_mix_post), (V_FFN_PRE, 2, g_ffn_pre),
                    (V_FFN_POST, 2, g_ffn_post),
                    (V_PW1B, 2, conv_pw1_b.rearrange("a (b d) -> (a b) d", b=2)), (V_DWB, 1, conv_dw_b),
                    (V_LNG, 1, conv_ln_g), (V_LNB, 1, conv_ln_b), (V_PW2B, 1, conv_pw2_b),
                    (V_DW, W, conv_dw_w[0])]
            for row, n, src in rows:
                sp.dma_start(vrows[row:row + n, :], src).then_inc(s["vec_loaded"], 16)
            for n in range(1):
                for r in range(2):
                    load(n, r, by_cols(conv_pw1_w[0], r, [(2 * n + r) * P, D + (2 * n + r) * P]))
            sp.wait_ge(s["zeroed"], 1)
            for g in range(4):
                sp.dma_start(bf[32 * g:32 * g + HEADS, :],
                             attn_b_f.rearrange("a h -> h a")).then_inc(s["wf_loaded"], 16)
            sp.dma_start(wfraw[:, :, :],
                         attn_w_in[0].rearrange("(k p) f -> p k f", p=P)[:, :, 3 * D:3 * D + HEADS]
                         ).then_inc(s["wf_loaded"], 16)
            with sp.Fori(1, 4) as i:
                for r in range(2):
                    load(N_PW1 + i, r, by_cols(conv_pw1_w[0], r, [i * 256 + r * P, i * 256 + (D + r * P)]))
            for i in range(2):
                for r in range(2):
                    load(N_PW2 + i, r, by_rows(conv_pw2_w[0], r, (2 * i + r) * 2 * P))

            def mlp_loads(l, n0):
                for half in range(2):
                    with sp.Fori(0, 4) as i:
                        for r in range(2):
                            load(n0 + 8 * half + i, r,
                                 by_rows(mlp_w_up[l], r, i * 512 + (half * 2048 + r * 256)))
                    with sp.Fori(0, 4) as i:
                        for r in range(2):
                            rows_ = mlp_w_down[l, half * 2048 + r * D:half * 2048 + (r + 1) * D, :]
                            load(n0 + 8 * half + 4 + i, r, by_rows(rows_, r, i * 256))

            mlp_loads(0, N_MLP0)
            wv = attn_w_in[0].rearrange("(k p) f -> p k f", p=P)
            with sp.Fori(0, PAIRS) as i:
                load(N_ATT + i, 0, by_cols(attn_w_in[0], 0, [i * P, i * P + D]))
                load(N_ATT + i, 1, [(wraw[:, 1, 4 * k:4 * k + 4, 0:P],
                                     wv[:, 4 * k:4 * k + 4, ds(i * P + 2 * D, P)]) for k in range(2)])
            for i in range(2):
                for r in range(2):
                    load(N_WO + i, r, by_rows(attn_w_o[0], r, (2 * i + r) * 2 * P))
            mlp_loads(1, N_MLP1)
            od = out[0].rearrange("(q p) d -> p q d", p=P)
            for k in range(0, KB, 2):
                sp.wait_ge(s["out_copied"], k + 2)
                sp.dma_start(od[:, :, k * P:(k + 2) * P],
                             outsb[:, :, k * P:(k + 2) * P]).then_inc(s["stored"], 16)
            sp.wait_ge(s["stored"], 16 * (KB // 2))

        @block.gpsimd
        def _(pool):
            g = nc.gpsimd
            g.memset(bf[:, :], 0.0).then_inc(s["zeroed"], 1)
            g.memset(ident[:, :], 0.0).then_inc(s["consts"], 1)
            g.memset(ones[:, :], 1.0).then_inc(s["consts"], 1)
            g.memset(eps[:, 0:1], RMS_EPS).then_inc(s["consts"], 1)
            g.memset(eps[:, 1:2], LN_EPS).then_inc(s["consts"], 1)
            pool.wait_ge(s["consts"], 1)
            g.affine_select(out=ident[:, :], in_=ident[:, :], compare_op=ALU.not_equal, fill=1.0, base=0,
                            pattern=[[-1, P]], channel_multiplier=1).then_inc(s["consts"], 1)
            g.memset(upad[:, :, :], 0.0).then_inc(s["consts"], 1)
            g.memset(onehot[:, :], 0.0).then_inc(s["sel"], 1)
            for q in range(4):
                pool.wait_ge(s["sel"], q + 1)
                g.affine_select(out=onehot[:, :], in_=onehot[:, :], compare_op=ALU.not_equal, fill=1.0,
                                base=-32 * q, pattern=[[-1, HEADS]],
                                channel_multiplier=1).then_inc(s["sel"], 1)
            pool.wait_ge(s["consts"], 6)
            pool.wait_ge(s["dw_lo"], 1)
            def diagonals(j, r):
                idb = ident[:, :].rearrange("p (a c) -> p a c", a=1).broadcast_to([P, PE_TAPS, P])
                for dst, src in ((diaghi, dwhi), (diaglo, dwlo)):
                    col = (src[:, j, :] if isinstance(j, int) else flat(src[:, ds(j, 1), :])).bitcast(F32)
                    col = col.rearrange("p (a c) -> p a c", c=1).broadcast_to([P, PE_TAPS, P])
                    g.tensor_tensor(dst[:, r, :, :], idb, col, ALU.mult).then_inc(s["diag"], 1)

            def y_total(j):
                pool.wait_ge(s["y_done"], j + 1)
                pool.wait_ge(s["y_sum"], j + 1)
                yb = blk(y, j)
                g.tensor_tensor(sumsq[:, :], sumsq[:, :], yb, ALU.add).then_inc(s["y_sum"], 1)

            for r in range(2):
                diagonals(r, r)
            pool.wait_ge(s["rinv_done"], 1)
            g.memset(sumsq[:, :], 0.0).then_inc(s["y_sum"], 1)
            with pool.Fori(0, 3) as i:
                for r in range(2):
                    pool.wait_ge(s["conv_done"], 2 * i + r + 1)
                    diagonals(2 * i + (2 + r), r)
                    y_total(2 * i + r)
            for j in range(6, KB):
                y_total(j)

            pool.wait_ge(unit[1], 2 * (N_MLP0 + 15) + 4)
            g.memset(wfhi[:, :, :].bitcast(F32), 0.0).then_inc(s["wf_zero"], 1)
            g.memset(wflo[:, :, :].bitcast(F32), 0.0).then_inc(s["wf_zero"], 1)
            pool.wait_ge(s["wf_loaded"], 80)
            pool.wait_ge(s["wf_zero"], 2)
            wsrc = wfraw[:, :, :]
            for q in range(4):
                g.tensor_copy(wfhi[:, :, 32 * q:32 * q + HEADS], wsrc).then_inc(s["wf_hi"], 1)
                pool.wait_ge(s["wf_hi"], q + 1)
                g.tensor_tensor(wflo[:, :, 32 * q:32 * q + HEADS], wsrc,
                                wfhi[:, :, 32 * q:32 * q + HEADS].bitcast(F32),
                                ALU.subtract).then_inc(s["wf_ready"], 1)
            g.memset(kzhi[:, :, :].bitcast(F32), 0.0).then_inc(s["f_base"], 1)
            g.memset(kzlo[:, :, :].bitcast(F32), 0.0).then_inc(s["f_base"], 1)
            g.memset(rhsF[:, :].bitcast(F32), 1.0).then_inc(s["f_base"], 1)
            g.memset(lhsB[:, :], 1.0).then_inc(s["f_base"], 1)
            g.memset(causal[:, :], 0.0).then_inc(s["f_base"], 1)
            pool.wait_ge(s["f_base"], 5)
            g.affine_select(out=causal[:, S - P:S], in_=causal[:, S - P:S], compare_op=ALU.is_ge,
                            fill=MASK, base=0, pattern=[[-1, P]],
                            channel_multiplier=1).then_inc(s["f_base"], 1)
            pool.wait_ge(s["f_rows"], 4)
            def head_rows(h, hh):
                oh = onehot[:, h:h + 1] if isinstance(h, int) else onehot[:, ds(h, 1)]
                g.tensor_tensor(lhsF[:, hh, :], lhsB[:, :], oh.broadcast_to([P, S]),
                                ALU.mult).then_inc(s["f_ready"], 1)
            pool.wait_ge(s["sel"], 5)
            for hh in range(2):
                head_rows(hh, hh)
            with pool.Fori(1, PAIRS) as p:
                for hh in range(2):
                    pool.wait_ge(s["sc_done"], 8 * p + (4 * hh - 4))
                    head_rows(2 * p + hh, hh)

        @block.tensor
        def _(pe):
            pe.sem_inc(unit[0], 2)
            pe.sem_inc(unit[1], 2)
            pe.sem_inc(s["t_done"], 8)
            pe.sem_inc(s["pv_done"], 1)

            def product(bank, u, kb, xhi, xlo, start, stop, cols=None):
                o = psum[:, bank, :]
                pe.matmul(o, whi[:, u, kb, :], xhi, start=start, stop=False)
                pe.matmul(o, whi[:, u, kb, :], xlo, start=False, stop=False)
                return pe.matmul(o, wlo[:, u, kb, :], xhi, start=False, stop=stop)

            def weights(n, u):
                pe.wait_ge(w_ready[u // 2], 2 * n + (1 + u % 2))

            def first_step(n, ready, count, units=4, xh=hhi, xl=hlo):
                for u in range(units):
                    weights(n, u)
                for kb in range(KB - 2):
                    pe.wait_ge(ready, count + kb + 1)
                    for u in range(units):
                        product(u, u, kb, xh[:, kb, :], xl[:, kb, :], kb == 0, False)
                pe.wait_ge(ready, count + KB)
                for u in range(units):
                    for kb in (KB - 2, KB - 1):
                        mm = product(u, u, kb, xh[:, kb, :], xl[:, kb, :], False, kb == KB - 1)
                    mm.then_inc(unit[u // 2], 2 if units == 3 and u == 2 else 1)

            def whole_unit(n, u, xh=hhi, xl=hlo):
                weights(n, u)
                for kb in range(KB):
                    mm = product(u, u, kb, xh[:, kb, :], xl[:, kb, :], kb == 0, kb == KB - 1)
                mm.then_inc(unit[u // 2], 1)

            def stat(sem, count):
                pe.wait_ge(sem, count)
                pe.matmul(psum[:, STAT, :], ones[:, :], sumsq[:, :], start=True,
                          stop=True).then_inc(s["stat"], 1)

            pe.wait_ge(s["consts"], 6)
            pe.wait_ge(s["vec_loaded"], 160)
            for k in range(KB):
                t = pe.transpose(psum[:, 7, k * V_ROWS:(k + 1) * V_ROWS], vrows[0:V_ROWS, k * P:(k + 1) * P],
                                 ident[0:V_ROWS, 0:V_ROWS])
            t.then_inc(s["vt_done"], 1)
            pe.wait_ge(s["x_loaded"], 16 * TB)
            for k in range(KB):
                if k >= 2:
                    pe.wait_ge(s["xt_copied"], k - 1)
                for q in range(TB):
                    t = pe.transpose(psum[:, 4 + k % 2, q * P:(q + 1) * P], xin[:, q, k * P:(k + 1) * P],
                                     ident[:, :])
                t.then_inc(s["xt_done"], 1)

            def conv(j, r):
                pe.wait_ge(s["u_ready"], j + 1)
                pe.wait_ge(s["diag"], 2 * j + 2)
                if not (isinstance(j, int) and j < 2):
                    pe.wait_ge(s["y_done"], j - 1)
                o = psum[:, 4 + r, :]
                for k in range(PE_TAPS):
                    t = DVE_TAPS + k
                    dh, dl = diaghi[:, r, k, :], diaglo[:, r, k, :]
                    xh, xl = uhi[:, r, t:t + S], ulo[:, r, t:t + S]
                    pe.matmul(o, dh, xh, start=k == 0, stop=False)
                    pe.matmul(o, dh, xl, start=False, stop=False)
                    mm = pe.matmul(o, dl, xh, start=False, stop=k == PE_TAPS - 1)
                mm.then_inc(s["conv_done"], 1)

            first_step(N_PW1, s["h_ready"], 0)
            stat(s["p_sum"], KB)
            conv(0, 0)
            with pe.Fori(1, 4) as i:
                for r in range(2):
                    pe.wait_ge(s["glu_u"], 2 * i + (r - 1))
                    for u in (2 * r, 2 * r + 1):
                        whole_unit(N_PW1 + i, u)
                    conv(2 * i + (r - 1), 1 - r)
            conv(7, 1)
            stat(s["y_sum"], KB + 1)
            stat(s["c_sum"], KB)

            first_step(N_PW2, s["c_ready"], 0)
            for u in range(4):
                pe.wait_ge(s["m_done"], u + 3)
                whole_unit(N_PW2 + 1, u)
            stat(s["m_sum"], 2 + KB)

            def mlp(l, n0, v, b):
                for half in range(2):
                    q = 2 * l + half
                    if half == 0:
                        first_step(n0, s["h_ready"], KB * v)
                        stat(s["p_sum"], KB * (v + 1))
                        i0 = 1
                    else:
                        i0 = 0
                    with pe.Fori(i0, 4) as i:
                        for u in range(4):
                            if q > 0 or i0 == 1:
                                pe.wait_ge(s["up_evac"], 4 * i + (16 * q - 4 + u + 1))
                            whole_unit(n0 + 8 * half + i, u)
                    if half == 1:
                        pe.wait_ge(s["dn_evac"], 8 * (l + 1) + 2)
                    with pe.Fori(0, 4) as i:
                        n = n0 + 8 * half + 4 + i
                        for u in range(4):
                            kg, f = u // 2, u % 2
                            weights(n, u)
                            pe.wait_ge(s["a_ready"], 16 * q + 8 * (kg + 1))
                            if kg == 0 and half == 0:
                                pe.wait_ge(s["dn_evac"], 2 * i + (8 * l + f + 1))
                            if kg == 0 and half == 1:
                                pe.wait_ge(s["m_done"], 2 * i + (8 * b + f + 1))
                            for kb in range(KB):
                                a = 8 * kg + kb
                                mm = product(4 + f, u, kb, ahi[:, a, :], alo[:, a, :],
                                             kg == 0 and kb == 0, kg == 1 and kb == KB - 1)
                            mm.then_inc(unit[u // 2], 1)
                stat(s["m_sum"], 2 + KB * (b + 1))

            mlp(0, N_MLP0, 1, 1)

            first_step(N_ATT, s["h_ready"], 2 * KB, units=3)
            pe.wait_ge(s["wf_ready"], 4)
            for kb in range(KB):
                o = psum[:, 3, :]
                pe.matmul(o, wfhi[:, kb, :], hhi[:, kb, :], start=kb == 0, stop=False)
                pe.matmul(o, wfhi[:, kb, :], hlo[:, kb, :], start=False, stop=False)
                mm = pe.matmul(o, wflo[:, kb, :], hhi[:, kb, :], start=False, stop=kb == KB - 1)
            mm.then_inc(s["f_done"], 1)
            stat(s["p_sum"], 3 * KB)

            def attention(p, project):
                for what, i in SEQ:
                    hh, j = i // 4, i % 4
                    if what == "S":
                        if i == 0:
                            pe.wait_ge(s["q_ready"], p + 1)
                            pe.wait_ge(s["k_ready"], 2 * p + 2)
                        if j == 0:
                            pe.wait_ge(s["f_ready"], 2 * p + (hh + 1))
                        pe.wait_ge(s["sc_evac"], 8 * p + (i + 1))
                        n = P * (j + 1)
                        o = psum[:, SCORE + i % 2, 0:n]
                        qb = slice(j * P, (j + 1) * P)
                        pe.matmul(o, lhsF[:, hh, qb], rhsF[:, 0:n], start=True, stop=False)
                        pe.matmul(o, qhi[:, qb], kzhi[:, hh, 0:n], start=False, stop=False)
                        pe.matmul(o, qhi[:, qb], kzlo[:, hh, 0:n], start=False, stop=False)
                        pe.matmul(o, qlo[:, qb], kzhi[:, hh, 0:n], start=False,
                                  stop=True).then_inc(s["sc_done"], 1)
                    if what == "V":
                        pe.wait_ge(s["pr_evac"], 3 * p + 6)
                        for q in range(TB):
                            t = pe.transpose(psum[:, 3, q * P:(q + 1) * P], tmp[:, 2, q * P:(q + 1) * P],
                                             ident[:, :])
                        t.then_inc(s["vtr"], 1)
                    if what == "P" and project:
                        u, part = i // 4, i % 4
                        n = N_ATT + 1 + p
                        if part == 0:
                            weights(n, u) if u < 2 else pe.wait_ge(w_ready[1], 2 * n + 2)
                            pe.wait_ge(s["pr_evac"], 3 * p + (3 + u + 1))
                        for kb in (2 * part, 2 * part + 1):
                            mm = product(u, u, kb, hhi[:, kb, :], hlo[:, kb, :], kb == 0, kb == KB - 1)
                        if part == 3:
                            mm.then_inc(unit[u // 2], 2 if u == 2 else 1)
                    if what == "T":
                        pe.wait_ge(s["p_ready"], 8 * p + (i + 1))
                        pe.wait_ge(s["pt_ready"], 8 * p + (i + 1))
                        pr = probs(hh, j)
                        for kb in range(j + 1):
                            t = pe.transpose(psum[:, TRP, kb * P:(kb + 1) * P], pr[:, kb * P:(kb + 1) * P],
                                             ident[:, :])
                        t.then_inc(s["t_done"], 1)
                    if what == "O":
                        pe.wait_ge(s["v_ready"], p + 1)
                        pe.wait_ge(s["pt_ready"], 8 * p + (4 * i + 5))
                        pe.wait_ge(s["o_ready"], 2 * p + (i + 1))
                        for kb in range(TB):
                            o = psum[:, OUTP, kb * P:S]
                            ph, pl = pThi[:, kb, kb * P:S], pTlo[:, kb, kb * P:S]
                            pe.matmul(o, vhi[:, kb, :], ph, start=kb == 0, stop=False)
                            pe.matmul(o, vhi[:, kb, :], pl, start=False, stop=False)
                            mm = pe.matmul(o, vlo[:, kb, :], ph, start=False, stop=kb == TB - 1)
                        mm.then_inc(s["pv_done"], 1)

            with pe.Fori(0, PAIRS - 2) as p:
                attention(p, True)
            attention(PAIRS - 2, True)
            attention(PAIRS - 1, False)

            pe.wait_ge(s["o_ready"], 2 * PAIRS + 1)
            for i in range(2):
                for u in range(4):
                    if i == 1:
                        pe.wait_ge(s["m_done"], 16 + u + 3)
                    whole_unit(N_WO + i, u, ohi, olo)
            stat(s["m_sum"], 2 + 3 * KB)
            mlp(1, N_MLP1, 3, 3)
            for k in range(KB):
                pe.wait_ge(s["x_done"], 3 * KB + k + 1)
                if k >= 2:
                    pe.wait_ge(s["out_copied"], k - 1)
                for q in range(TB):
                    t = pe.transpose(psum[:, k % 2, q * P:(q + 1) * P], xT[:, k, q * P:(q + 1) * P],
                                     ident[:, :])
                t.then_inc(s["out_tr"], 1)

        @block.scalar
        def _(act):
            a = nc.scalar

            def split_hi(n, u, single=False):
                r, c = u // 2, u % 2
                act.wait_ge(raw[r], 32 * n + 32)
                act.wait_ge(unit[r], 2 * n + (2 if single else 1 + c))
                a.activation(whi[:, u, :, :], wraw[:, r, :, c * P:(c + 1) * P],
                             ACT.Copy).then_inc(w_hi[r], 2 if single else 1)

            def done(n, u):
                act.wait_ge(unit[u // 2], 2 * n + (3 + u % 2))

            def square(src, k, sem_in, count, sem_free, free, sem_out):
                act.wait_ge(sem_in, count)
                if free is not None:
                    act.wait_ge(sem_free, free)
                a.activation(tmp[:, 2 + k % 2, :], src, ACT.Square).then_inc(sem_out, 1)

            def pre_norm(v, row, x_sem, x_count):
                for k in range(KB):
                    act.wait_ge(x_sem, x_count + k + 1)
                    a.activation(hhi[:, k, :], xT[:, k, :], ACT.Identity,
                                 scale=vcol(row, k)).then_inc(s["h_hi"], 1)
                    square(xT[:, k, :], k, x_sem, x_count + k + 1, s["p_sum"],
                           KB * v + k - 1 if KB * v + k > 1 else None, s["p_sq"])

            def root(idx, e=0):
                act.wait_ge(s["stat"], idx + 1)
                a.activation(rinv[:, :], psum[:, STAT, :], ACT.Sqrt, scale=1.0 / D,
                             bias=eps[:, e:e + 1]).then_inc(s["root"], 1)

            for u in range(4):
                split_hi(0, u)
            act.wait_ge(s["vec_ready"], 1)
            a.activation(dwhi[:, :, :], vec[:, :, V_DW + DVE_TAPS:V_DW + W],
                         ACT.Copy).then_inc(s["dw_hi"], 1)
            pre_norm(0, V_MIX_PRE, s["xt_copied"], 0)
            root(ST_PRE0)

            def gates(j, r):
                act.wait_ge(s["glu_g"], j + 1)
                a.activation(tmp[:, 1, :], tmp[:, 0, :], ACT.Sigmoid, bias=vcol(V_PW1B + 1, j)
                             ).then_inc(s["glu_s"], 1)
                act.wait_ge(s["glu_u"], j + 1)
                if not (isinstance(j, int) and j < 2):
                    act.wait_ge(s["conv_done"], j - 1)
                a.activation(uhi[:, r, :], upad[:, r, :], ACT.Copy).then_inc(s["u_hi"], 1)

            def conv_step(n):
                for r in range(2):
                    gates(2 * n + r, r)
                    for c in range(2):
                        split_hi(n + 1, 2 * r + c)
            conv_step(0)
            with act.Fori(1, 4) as i:
                conv_step(i)
            act.wait_ge(s["stat"], ST_MEAN + 1)
            a.activation(rinv[:, :], psum[:, STAT, :], ACT.Copy, scale=1.0 / D).then_inc(s["root"], 1)
            for k in range(KB):
                square(y[:, k, :], k, s["c_sub"], k + 1, s["c_sum"], k - 1 if k > 1 else None, s["c_sq"])
            root(ST_VAR, 1)
            for k in range(KB):
                act.wait_ge(s["c_nrm"], k + 1)
                if k >= 2:
                    act.wait_ge(s["c_ready"], k - 1)
                a.activation(tmp[:, k % 2, :], y[:, k, :], ACT.Silu, scale=vcol(V_LNG, k),
                             bias=vcol(V_LNB, k)).then_inc(s["c_silu"], 1)
                act.wait_ge(s["c_silu"], k + 1)
                a.activation(hhi[:, k, :], tmp[:, k % 2, :], ACT.Copy).then_inc(s["c_hi"], 1)

            def mixer_out(n0, b, dst, bias_row):
                for i in range(2):
                    for u in range(4):
                        k = 4 * i + u
                        done(n0 + i, u)
                        if bias_row is None:
                            e = a.activation(dst[:, k, :], psum[:, u, :], ACT.Copy)
                        else:
                            e = a.activation(dst[:, k, :], psum[:, u, :], ACT.Identity,
                                             bias=vcol(bias_row, k))
                        e.then_inc(s["m_done"], 1)
                        square(dst[:, k, :], k, s["m_done"], KB * b + k + 3, s["m_sum"],
                               KB * b + k + 1, s["m_sq"])
                        split_hi(n0 + i + 1, u)
                root(ST_POST[b])

            mixer_out(N_PW2, 0, m, V_PW2B)

            def mlp(l, n0, b, last):
                v = 1 if l == 0 else 3
                pre_norm(v, V_FFN_PRE + l, s["x_done"], KB * (b - 1))
                root(ST_PRE[v])
                for half in range(2):
                    q = 2 * l + half
                    def up(i):
                        for u in range(4):
                            act.wait_ge(s["up_sq"], 4 * i + (16 * q + u + 1))
                            a.activation(blk(ahi, 4 * i + u), tmp[:, 2 + u % 2, :],
                                         ACT.Copy).then_inc(s["up_hi"], 1)
                            split_hi(n0 + 8 * half + i + 1, u)
                    with act.Fori(0, 4) as i:
                        up(i)
                    nd = n0 + 8 * half + 4
                    def down(i, split):
                        for u in range(4):
                            if u >= 2:
                                f = u - 2
                                if half == 0:
                                    done(nd + i, u)
                                    a.activation(blk(m, 2 * i + f), psum[:, 4 + f, :],
                                                 ACT.Copy).then_inc(s["dn_evac"], 1)
                                else:
                                    square(blk(m, 2 * i + f), f, s["m_done"], 2 * i + (KB * b + f + 3),
                                           s["m_sum"], 2 * i + (KB * b + f + 1), s["m_sq"])
                            if split:
                                split_hi(nd + i + 1, u)
                    with act.Fori(0, 3) as i:
                        down(i, True)
                    if half == 0:
                        down(3, True)
                    elif last:
                        down(3, False)
                    else:
                        for u in range(4):
                            if u >= 2:
                                f = u - 2
                                square(m[:, 6 + f, :], f, s["m_done"], 6 + KB * b + f + 3,
                                       s["m_sum"], 6 + KB * b + f + 1, s["m_sq"])
                            if u < 3:
                                split_hi_att(N_ATT, u)
                root(ST_POST[b])

            def split_hi_att(n, u):
                split_hi(n, u, single=u == 2)

            a.sem_inc(s["dn_evac"], 2)
            mlp(0, N_MLP0, 1, False)
            pre_norm(2, V_MIX_PRE + 1, s["x_done"], KB)
            root(ST_PRE[2])

            def q_hi(p):
                act.wait_ge(s["pr_evac"], 3 * p + 4)
                if not (isinstance(p, int) and p == 0):
                    act.wait_ge(s["sc_done"], 8 * p)
                a.activation(qhi[:, :], tmp[:, 0, :], ACT.Copy).then_inc(s["q_hi"], 1)

            def k_hi(p):
                act.wait_ge(s["pr_evac"], 3 * p + 5)
                for hh in range(2):
                    rows = slice(HD * hh, HD * hh + HD)
                    a.activation(kzhi[rows, hh, :], tmp[rows, 1, :], ACT.Copy).then_inc(s["k_hi"], 1)

            q_hi(0)
            split_hi_att(N_ATT + 1, 0)
            act.wait_ge(s["f_base"], 6)
            k_hi(0)
            split_hi_att(N_ATT + 1, 1)
            split_hi_att(N_ATT + 1, 2)
            act.wait_ge(s["f_abs"], 1)
            a.activation(fwork[:, FEXP, :], fwork[:, FABS, :], ACT.Exp, scale=-1.0).then_inc(s["f_exp"], 1)
            act.wait_ge(s["f_exp"], 1)
            a.activation(fwork[:, FLN, :], fwork[:, FEXP, :], ACT.Ln, bias=1.0).then_inc(s["f_ln"], 1)
            act.wait_ge(s["f_cum"], 1)
            a.activation(Fhi[:, :], fwork[:, FCUM, :], ACT.Copy).then_inc(s["f_hi"], 1)
            act.wait_ge(s["f_hi"], 1)
            a.activation(rhsF[0:HEADS, :], Fhi[0:HEADS, :].bitcast(F32), ACT.Copy).then_inc(s["f_rows"], 1)
            a.activation(lhsB[64:64 + HEADS, :], Fhi[64:64 + HEADS, :].bitcast(F32), ACT.Copy,
                         scale=-1.0).then_inc(s["f_rows"], 1)

            def attention(p, project, units):
                for what, i in SEQ:
                    hh, j = i // 4, i % 4
                    if what == "S":
                        act.wait_ge(s["sc_evac"], 8 * p + (i + 3))
                        pr = probs(hh, j)
                        a.activation(pr, pr, ACT.Exp, scale=-1.0, bias=negmax[:, i:i + 1],
                                     accum_out=den[:, i:i + 1]).then_inc(s["ex_done"], 1)
                    if what == "V":
                        act.wait_ge(s["vtr"], p + 1)
                        act.wait_ge(s["pv_done"], 2 * p + 1)
                        a.activation(flat(vhi[:, :, :]), psum[:, 3, :], ACT.Copy).then_inc(s["v_hi"], 1)
                    if what == "P" and project:
                        n = N_ATT + 2 + p
                        if i == 3:
                            q_hi(p + 1)
                        if i == 7:
                            k_hi(p + 1)
                        if i % 4 == 3:
                            u = i // 4
                            if units == 3:
                                split_hi_att(n, u)
                            else:
                                split_hi(n, u)
                                if u == 2:
                                    split_hi(n, 3)
                    if what == "T":
                        act.wait_ge(s["t_done"], 8 * p + (i + 9))
                        if j == 0:
                            act.wait_ge(s["pv_done"], 2 * p + (hh + 1))
                        src = psum[:, TRP, 0:(j + 1) * P].rearrange("p (a b) -> p a b", b=P)
                        a.activation(pThi[:, 0:j + 1, j * P:(j + 1) * P], src,
                                     ACT.Copy).then_inc(s["p_hi"], 1)
                    if what == "O":
                        act.wait_ge(s["pv_done"], 2 * p + (i + 2))
                        rows = slice(HD * i, HD * i + HD)
                        dst = ohi[rows, p, :] if isinstance(p, int) else flat(ohi[rows, ds(p, 1), :])
                        a.activation(dst, psum[rows, OUTP, :], ACT.Copy).then_inc(s["o_hi"], 1)

            with act.Fori(0, PAIRS - 2) as p:
                attention(p, True, 3)
            attention(PAIRS - 2, True, 4)
            attention(PAIRS - 1, False, 0)
            mixer_out(N_WO, 2, m_wo, None)
            mlp(1, N_MLP1, 3, True)

        @block.vector
        def _(dve):
            d = nc.vector

            def split_lo(n, u, single=False):
                r, c = u // 2, u % 2
                dve.wait_ge(w_hi[r], 2 * n + (2 if single else 1 + c))
                d.tensor_tensor(wlo[:, u, :, :], wraw[:, r, :, c * P:(c + 1) * P],
                                whi[:, u, :, :].bitcast(F32), ALU.subtract
                                ).then_inc(w_ready[r], 2 if single else 1)

            def done(n, u):
                dve.wait_ge(unit[u // 2], 2 * n + (3 + u % 2))

            def h_lo(v, row, k):
                dve.wait_ge(s["h_hi"], KB * v + k + 1)
                d.scalar_tensor_tensor(hlo[:, k, :], xT[:, k, :], vcol(row, k), hhi[:, k, :].bitcast(F32),
                                       ALU.mult, ALU.subtract).then_inc(s["h_ready"], 1)

            def add_square(k, sem_in, count, sem_out, prev):
                dve.wait_ge(sem_in, count)
                if k == 0:
                    d.tensor_copy(sumsq[:, :], tmp[:, 2 + k % 2, :]).then_inc(sem_out, 1)
                else:
                    dve.wait_ge(sem_out, prev)
                    d.tensor_tensor(sumsq[:, :], sumsq[:, :], tmp[:, 2 + k % 2, :],
                                    ALU.add).then_inc(sem_out, 1)

            def inverse(idx):
                dve.wait_ge(s["root"], idx + 1)
                d.reciprocal(rinv[:, :], rinv[:, :]).then_inc(s["rinv_done"], 1)

            def inverse_ready(idx):
                dve.wait_ge(s["rinv_done"], idx + 1 if idx < ST_MEAN else idx)

            d.sem_inc(s["m_done"], 2)
            d.sem_inc(s["m_sum"], 2)
            d.sem_inc(s["sc_evac"], 2)
            d.sem_inc(s["pt_ready"], 1)
            d.sem_inc(s["o_ready"], 1)
            d.sem_inc(s["pr_evac"], 3)
            dve.wait_ge(s["vt_done"], 1)
            d.tensor_copy(flat(vec[:, :, :]), psum[:, 7, 0:KB * V_ROWS]).then_inc(s["vec_ready"], 1)
            dve.wait_ge(s["dw_hi"], 1)
            d.tensor_tensor(dwlo[:, :, :], vec[:, :, V_DW + DVE_TAPS:V_DW + W], dwhi[:, :, :].bitcast(F32),
                            ALU.subtract).then_inc(s["dw_lo"], 1)
            for k in range(KB + 1):
                if k < KB:
                    dve.wait_ge(s["xt_done"], k + 1)
                    d.tensor_copy(xT[:, k, :], psum[:, 4 + k % 2, :]).then_inc(s["xt_copied"], 1)
                if k >= 1:
                    h_lo(0, V_MIX_PRE, k - 1)
                    add_square(k - 1, s["p_sq"], k, s["p_sum"], k - 1)
                if k % 2 == 0 and k < KB:
                    split_lo(0, k // 2)
            inverse(ST_PRE0)

            def tap(j, r, t):
                g = DVE_TAPS * j + t
                dst = blk(y, j) if t % 2 == 0 else acc1[:, :]
                src = upad[:, r, t:t + S]
                if t == 0:
                    i = d.tensor_scalar(dst, src, vcol(V_DW, j), vcol(V_DWB, j), ALU.mult, ALU.add)
                elif t == 1:
                    i = d.tensor_scalar(dst, src, vcol(V_DW + 1, j), None, ALU.mult)
                else:
                    dve.wait_ge(s["tap"], g - 1)
                    i = d.scalar_tensor_tensor(dst, src, vcol(V_DW + t, j), dst, ALU.mult, ALU.add)
                i.then_inc(s["tap"], 1)

            def conv_block(n, r):
                j = 2 * n + r
                if isinstance(j, int) and j == 0:
                    inverse_ready(ST_PRE0)
                done(N_PW1 + n, 2 * r + 1)
                if not (isinstance(j, int) and j == 0):
                    dve.wait_ge(s["glu_u"], j)
                d.tensor_tensor(tmp[:, 0, :], psum[:, 2 * r + 1, :], rinv[:, :],
                                ALU.mult).then_inc(s["glu_g"], 1)
                d.tensor_tensor(tmp[:, 2, :], psum[:, 2 * r, :], rinv[:, :],
                                ALU.mult).then_inc(s["glu_t"], 1)
                dve.wait_ge(s["glu_t"], j + 1)
                dve.wait_ge(s["glu_s"], j + 1)
                if isinstance(j, int) and j < 2:
                    dve.wait_ge(s["consts"], 6)
                else:
                    dve.wait_ge(s["u_ready"], j - 1)
                d.scalar_tensor_tensor(upad[:, r, W - 1:W - 1 + S], tmp[:, 2, :], vcol(V_PW1B, j),
                                       tmp[:, 1, :], ALU.add, ALU.mult).then_inc(s["glu_u"], 1)
                dve.wait_ge(s["glu_u"], j + 1)
                tap(j, r, 0)
                if not (isinstance(j, int) and j == 0):
                    dve.wait_ge(s["y_done"], j)
                tap(j, r, 1)
                dve.wait_ge(s["u_hi"], j + 1)
                d.tensor_tensor(ulo[:, r, :], upad[:, r, :], uhi[:, r, :].bitcast(F32),
                                ALU.subtract).then_inc(s["u_ready"], 1)
                for t in range(2, DVE_TAPS):
                    tap(j, r, t)
                    if t == DVE_TAPS // 2:
                        split_lo(n + 1, 2 * r)
                split_lo(n + 1, 2 * r + 1)
                dve.wait_ge(s["tap"], DVE_TAPS * (j + 1))
                d.tensor_tensor(acc1[:, :], acc1[:, :], blk(y, j), ALU.add).then_inc(s["acc"], 1)
                dve.wait_ge(s["acc"], j + 1)
                dve.wait_ge(s["conv_done"], j + 1)
                d.tensor_tensor(blk(y, j), psum[:, 4 + r, :], acc1[:, :], ALU.add
                                ).then_inc(s["y_done"], 1)

            def conv_step(n):
                for r in range(2):
                    conv_block(n, r)
            conv_step(0)
            with dve.Fori(1, 4) as i:
                conv_step(i)
            dve.wait_ge(s["root"], ST_MEAN + 1)
            for k in range(KB + 1):
                if k < KB:
                    d.tensor_tensor(y[:, k, :], y[:, k, :], rinv[:, :], ALU.subtract).then_inc(s["c_sub"], 1)
                if k >= 1:
                    add_square(k - 1, s["c_sq"], k, s["c_sum"], k - 1)
            inverse(ST_VAR)
            inverse_ready(ST_VAR)
            for k in range(KB + 1):
                if k < KB:
                    d.tensor_tensor(y[:, k, :], y[:, k, :], rinv[:, :], ALU.mult).then_inc(s["c_nrm"], 1)
                if k >= 1:
                    dve.wait_ge(s["c_hi"], k)
                    d.tensor_tensor(hlo[:, k - 1, :], tmp[:, (k - 1) % 2, :], hhi[:, k - 1, :].bitcast(F32),
                                    ALU.subtract).then_inc(s["c_ready"], 1)

            def mixer_out(n0, b):
                for i in range(2):
                    for u in range(4):
                        k = 4 * i + u
                        add_square(k, s["m_sq"], KB * b + k + 1, s["m_sum"], KB * b + k + 2)
                        split_lo(n0 + i + 1, u)

            def boundary(b, row_post, v, row_pre):
                inverse(ST_POST[b])
                inverse_ready(ST_POST[b])
                src = mbuf(b)
                for k in range(KB + 1):
                    c = KB * b + k
                    if k < KB:
                        if c >= 2:
                            dve.wait_ge(s["x_done"], c - 1)
                        d.scalar_tensor_tensor(tmp[:, k % 2, :], src[:, k, :], vcol(row_post, k), rinv[:, :],
                                               ALU.mult, ALU.mult).then_inc(s["t1_done"], 1)
                        dve.wait_ge(s["t1_done"], c + 1)
                        d.tensor_tensor(xT[:, k, :], xT[:, k, :], tmp[:, k % 2, :],
                                        ALU.add).then_inc(s["x_done"], 1)
                    if k >= 1 and v is not None:
                        h_lo(v, row_pre, k - 1)
                        add_square(k - 1, s["p_sq"], KB * v + k, s["p_sum"], KB * v + k - 1)
                if v is not None:
                    inverse(ST_PRE[v])
                    inverse_ready(ST_PRE[v])

            mixer_out(N_PW2, 0)
            boundary(0, V_MIX_POST, 1, V_FFN_PRE)

            def mlp(l, n0, b, last):
                for half in range(2):
                    q = 2 * l + half
                    def a_lo(i, u):
                        dve.wait_ge(s["up_hi"], 4 * i + (16 * q + u + 1))
                        d.tensor_tensor(blk(alo, 4 * i + u), tmp[:, 2 + u % 2, :],
                                        blk(ahi, 4 * i + u).bitcast(F32),
                                        ALU.subtract).then_inc(s["a_ready"], 1)
                    def up(i, peeled):
                        n = n0 + 8 * half + i
                        for u in range(4):
                            c = 4 * i + (16 * q + u)
                            done(n, u)
                            if not (q == 0 and peeled and u == 0):
                                dve.wait_ge(s["up_sq"], c)
                            d.tensor_tensor(tmp[:, 0, :], psum[:, u, :], rinv[:, :],
                                            ALU.mult).then_inc(s["up_evac"], 1)
                            dve.wait_ge(s["up_evac"], c + 1)
                            if not (q == 0 and peeled and u < 2):
                                dve.wait_ge(s["a_ready"], c - 1)
                            d.scalar_tensor_tensor(tmp[:, 2 + u % 2, :], tmp[:, 0, :], 0.0, tmp[:, 0, :],
                                                   ALU.max, ALU.mult).then_inc(s["up_sq"], 1)
                            if u >= 1:
                                a_lo(i, u - 1)
                            split_lo(n + 1, u)
                        a_lo(i, 3)
                    up(0, True)
                    with dve.Fori(1, 4) as i:
                        up(i, False)
                    nd = n0 + 8 * half + 4
                    if half == 0:
                        with dve.Fori(0, 4) as i:
                            for u in range(4):
                                split_lo(nd + i + 1, u)
                        continue
                    d.memset(sumsq[:, :], 0.0).then_inc(s["m_zero"], 1)
                    dve.wait_ge(s["m_zero"], l + 1)
                    def add_sq(i, f):
                        dve.wait_ge(s["m_sq"], 2 * i + (KB * b + f + 1))
                        dve.wait_ge(s["m_sum"], 2 * i + (KB * b + f + 2))
                        d.tensor_tensor(sumsq[:, :], sumsq[:, :], tmp[:, 2 + f, :],
                                        ALU.add).then_inc(s["m_sum"], 1)
                    def down(i, units):
                        for u in range(4):
                            if u >= 2:
                                f = u - 2
                                done(nd + i, u)
                                mb = blk(m, 2 * i + f)
                                d.tensor_tensor(mb, psum[:, 4 + f, :], mb, ALU.add).then_inc(s["m_done"], 1)
                            if u == 3:
                                add_sq(i, 0)
                            if u < units:
                                split_lo(nd + i + 1, u, single=units == 3 and u == 2)
                        add_sq(i, 1)
                    dve.wait_ge(s["dn_evac"], 8 * (l + 1) + 2)
                    with dve.Fori(0, 3) as i:
                        down(i, 4)
                    down(3, 0 if last else 3)

            mlp(0, N_MLP0, 1, False)
            boundary(1, V_FFN_POST, 2, V_MIX_PRE + 1)

            def q_evac(p):
                n = N_ATT + p
                done(n, 0)
                if not (isinstance(p, int) and p == 0):
                    dve.wait_ge(s["q_ready"], p)
                d.scalar_tensor_tensor(tmp[:, 0, :], psum[:, 0, :], -HD ** -0.5, rinv[:, :], ALU.mult,
                                       ALU.mult).then_inc(s["pr_evac"], 1)

            def q_lo(p):
                dve.wait_ge(s["q_hi"], p + 1)
                d.tensor_tensor(qlo[:, :], tmp[:, 0, :], qhi[:, :].bitcast(F32),
                                ALU.subtract).then_inc(s["q_ready"], 1)

            def k_evac(p):
                done(N_ATT + p, 1)
                if not (isinstance(p, int) and p == 0):
                    dve.wait_ge(s["k_ready"], 2 * p)
                d.tensor_tensor(tmp[:, 1, :], psum[:, 1, :], rinv[:, :], ALU.mult).then_inc(s["pr_evac"], 1)

            def k_lo(p):
                for hh in range(2):
                    rows = slice(HD * hh, HD * hh + HD)
                    dve.wait_ge(s["k_hi"], 2 * p + (hh + 1))
                    d.tensor_tensor(kzlo[rows, hh, :], tmp[rows, 1, :], kzhi[rows, hh, :].bitcast(F32),
                                    ALU.subtract).then_inc(s["k_ready"], 1)

            def v_evac(p):
                dve.wait_ge(unit[1], 2 * (N_ATT + p) + 4)
                if not (isinstance(p, int) and p == 0):
                    dve.wait_ge(s["vtr"], p)
                d.tensor_tensor(tmp[:, 2, :], psum[:, 2, :], rinv[:, :], ALU.mult).then_inc(s["pr_evac"], 1)

            q_evac(0)
            split_lo(N_ATT + 1, 0)
            q_lo(0)
            k_evac(0)
            split_lo(N_ATT + 1, 1)
            k_lo(0)
            v_evac(0)
            split_lo(N_ATT + 1, 2, single=True)
            dve.wait_ge(s["f_done"], 1)
            d.tensor_tensor(fwork[:, FZ, :], psum[:, 3, :], rinv[:, :], ALU.mult).then_inc(s["f_z"], 1)
            dve.wait_ge(s["f_z"], 1)
            dve.wait_ge(s["wf_loaded"], 80)
            d.tensor_scalar(fwork[:, FB, :], fwork[:, FZ, :], bf[:, 0:1], None, ALU.add).then_inc(s["f_b"], 1)
            dve.wait_ge(s["f_b"], 1)
            d.scalar_tensor_tensor(fwork[:, FABS, :], fwork[:, FB, :], -1.0, fwork[:, FB, :], ALU.mult,
                                   ALU.max).then_inc(s["f_abs"], 1)
            d.memset(tmp[:, 3, :], 1.0).then_inc(s["f_log"], 1)
            dve.wait_ge(s["f_ln"], 1)
            d.scalar_tensor_tensor(fwork[:, FLOG, :], fwork[:, FB, :], 0.0, fwork[:, FLN, :], ALU.min,
                                   ALU.subtract).then_inc(s["f_log"], 1)
            dve.wait_ge(s["f_log"], 2)
            d.tensor_tensor_scan(fwork[:, FCUM, :], tmp[:, 3, :], fwork[:, FLOG, :], 0.0,
                                 ALU.mult, ALU.add).then_inc(s["f_cum"], 1)
            dve.wait_ge(s["f_hi"], 1)
            dve.wait_ge(s["f_base"], 6)
            d.tensor_tensor(fwork[:, FZ, :], fwork[:, FCUM, :], Fhi[:, :].bitcast(F32),
                            ALU.subtract).then_inc(s["f_lo"], 1)
            dve.wait_ge(s["f_lo"], 1)
            d.tensor_copy(rhsF[32:32 + HEADS, :], fwork[32:32 + HEADS, FZ, :]).then_inc(s["f_rows"], 1)
            d.tensor_scalar(lhsB[96:96 + HEADS, :], fwork[96:96 + HEADS, FZ, :], -1.0, None,
                            ALU.mult).then_inc(s["f_rows"], 1)

            def attention(p, project, units):
                def normalise(i):
                    hh, j = i // 4, i % 4
                    dve.wait_ge(s["ex_done"], 8 * p + (i + 1))
                    d.reciprocal(rden[:, i:i + 1], den[:, i:i + 1]).then_inc(s["rc_done"], 1)
                    dve.wait_ge(s["rc_done"], 8 * p + (i + 1))
                    pr = probs(hh, j)
                    d.tensor_scalar(pr, pr, rden[:, i:i + 1], None, ALU.mult).then_inc(s["p_ready"], 1)

                for what, i in SEQ:
                    hh, j = i // 4, i % 4
                    if what == "S":
                        dve.wait_ge(s["sc_done"], 8 * p + (i + 1))
                        dve.wait_ge(s["t_done"], 8 * p + (i + 1))
                        d.sem_inc(s["sc_seen"], 1)
                        d.tensor_tensor_reduce(out=probs(hh, j), in0=psum[:, SCORE + i % 2, 0:(j + 1) * P],
                                               in1=causal[:, S - (j + 1) * P:S], scale=1.0, scalar=3e38,
                                               op0=ALU.add, op1=ALU.min,
                                               accum_out=negmax[:, i:i + 1]).then_inc(s["sc_evac"], 1)
                        if i >= 1:
                            normalise(i - 1)
                        if i == 7:
                            normalise(7)
                    if what == "V":
                        dve.wait_ge(s["v_hi"], p + 1)
                        d.tensor_tensor(flat(vlo[:, :, :]), psum[:, 3, :], flat(vhi[:, :, :]).bitcast(F32),
                                        ALU.subtract).then_inc(s["v_ready"], 1)
                    if what == "P" and project and i % 4 == 3:
                        u, n = i // 4, N_ATT + 2 + p
                        if u == 0:
                            q_evac(p + 1)
                        if u == 1:
                            k_evac(p + 1)
                        if u == 2:
                            v_evac(p + 1)
                        split_lo(n, u, single=units == 3 and u == 2)
                        if units == 4 and u == 2:
                            split_lo(n, 3)
                        if u == 0:
                            q_lo(p + 1)
                        if u == 1:
                            k_lo(p + 1)
                    if what == "T":
                        dve.wait_ge(s["p_hi"], 8 * p + (i + 1))
                        src = psum[:, TRP, 0:(j + 1) * P].rearrange("p (a b) -> p a b", b=P)
                        d.tensor_tensor(pTlo[:, 0:j + 1, j * P:(j + 1) * P], src,
                                        pThi[:, 0:j + 1, j * P:(j + 1) * P].bitcast(F32),
                                        ALU.subtract).then_inc(s["pt_ready"], 1)
                    if what == "O":
                        dve.wait_ge(s["o_hi"], 2 * p + (i + 1))
                        rows = slice(HD * i, HD * i + HD)
                        if isinstance(p, int):
                            dst, hi = olo[rows, p, :], ohi[rows, p, :]
                        else:
                            dst, hi = flat(olo[rows, ds(p, 1), :]), flat(ohi[rows, ds(p, 1), :])
                        d.tensor_tensor(dst, psum[rows, OUTP, :], hi.bitcast(F32),
                                        ALU.subtract).then_inc(s["o_ready"], 1)

            with dve.Fori(0, PAIRS - 2) as p:
                attention(p, True, 3)
            attention(PAIRS - 2, True, 4)
            attention(PAIRS - 1, False, 0)
            mixer_out(N_WO, 2)
            boundary(2, V_MIX_POST + 1, 3, V_FFN_PRE + 1)
            mlp(1, N_MLP1, 3, True)
            boundary(3, V_FFN_POST + 1, None, None)
            for k in range(KB):
                dve.wait_ge(s["out_tr"], k + 1)
                d.tensor_copy(outsb[:, :, k * P:(k + 1) * P],
                              psum[:, k % 2, :].rearrange("p (q c) -> p q c", c=P)
                              ).then_inc(s["out_copied"], 1)


_INS = ["x", "g_mix_pre", "g_mix_post", "g_ffn_pre", "g_ffn_post", "conv_pw1_w", "conv_pw1_b",
        "conv_dw_w", "conv_dw_b", "conv_ln_g", "conv_ln_b", "conv_pw2_w", "conv_pw2_b", "attn_w_in",
        "attn_b_f", "attn_w_o", "mlp_w_up", "mlp_w_down"]


def kernel(**inputs):
    import numpy as np
    import concourse.bacc as bacc
    from concourse import mybir as mb
    from concourse.bass_utils import run_bass_kernel_spmd as run

    nc = bacc.Bacc("TRN2", target_bir_lowering=False, num_devices=1)
    arrays, args = {}, []
    for name in _INS:
        a = np.ascontiguousarray(inputs[name])
        arrays[f"in_{name}"] = a
        args.append(nc.dram_tensor(f"in_{name}", a.shape, mb.dt.from_np(a.dtype),
                                   kind="ExternalInput").ap())
    args.append(nc.dram_tensor("out_x", (1, S, D), F32, kind="ExternalOutput").ap())
    build(nc, *args)
    r = run(nc, [arrays], core_ids=[0])
    return r.results[0]["out_x"]
```

```python
import concourse.bass as bass
from concourse import mybir

F32 = mybir.dt.float32
F32R = mybir.dt.float32r
ALU = mybir.AluOpType
ACT = mybir.ActivationFunctionType
ds = bass.ds

P = 128
D = 1024
S = 512
KB = D // P
TB = S // P
FF = 4 * D
HEADS = 16
HD = D // HEADS
PAIRS = HEADS // 2
W = 31
PADW = S + W + 1
PE_TAPS = 12
DVE_TAPS = W - PE_TAPS
MASK = 1e30
RMS_EPS = 1e-6
LN_EPS = 1e-5

N_PW1 = 0
N_PW2 = N_PW1 + 4
N_MLP0 = N_PW2 + 2
N_ATT = N_MLP0 + 16
N_WO = N_ATT + PAIRS
N_MLP1 = N_WO + 2
STEPS = N_MLP1 + 16

V_MIX_PRE, V_MIX_POST, V_FFN_PRE, V_FFN_POST = 0, 2, 4, 6
V_PW1B, V_DWB, V_LNG, V_LNB, V_PW2B, V_DW = 8, 10, 11, 12, 13, 14
V_ROWS = V_DW + W

ST_PRE = ("pre0", "pre1", "pre2", "pre3")
ST_POST = ("post0", "post1", "post2", "post3")
ST_VAR = "var"
NTH = {name: n + 1 for n, name in enumerate(
    ["pre0", "var", "post0", "pre1", "post1", "pre2", "post2", "pre3", "post3"])}
RINV_NTH = {name: n + 1 for n, name in enumerate(["pre0", "pre1", "pre2", "pre3"])}

SEQ = [("P", 0), ("P", 1), ("S", 0), ("S", 1), ("V", 0), ("P", 2), ("S", 2), ("S", 3), ("P", 3),
       ("S", 4), ("S", 5), ("P", 4), ("S", 6), ("S", 7), ("P", 5), ("T", 0), ("P", 6), ("EVAC", 0),
       ("T", 1), ("PARTS", 0), ("T", 2), ("P", 7), ("SPLIT", 0), ("T", 3), ("P", 8), ("EVAC", 1),
       ("O", 0), ("T", 4), ("P", 9), ("PARTS", 1), ("T", 5), ("SPLIT", 1), ("T", 6), ("P", 10),
       ("T", 7), ("P", 11), ("O", 1), ("EVAC", 2), ("SPLIT", 2)]
PARTS_OF_P = 12

def build(nc, x, g_mix_pre, g_mix_post, g_ffn_pre, g_ffn_post, conv_pw1_w, conv_pw1_b, conv_dw_w,
          conv_dw_b, conv_ln_g, conv_ln_b, conv_pw2_w, conv_pw2_b, attn_w_in, attn_b_f, attn_w_o,
          mlp_w_up, mlp_w_down, out):
    at = [0]
    base = (nc.sbuf_base + 63) // 64 * 64
    nc.alloc_sbuf_tensor("slab", [P, (nc.sbuf_usable_end - nc.sbuf_base - 256) // 4], F32)

    def put(name, shape, dt, where=None):
        n = 4
        for s in shape[1:]:
            n *= s
        pos = at[0] if where is None else where[0]
        t = nc.alloc_sbuf_tensor_at(name, shape, dt, offset=base + pos)
        if where is None:
            at[0] += (n + 31) // 32 * 32
        else:
            where[0] += (n + 31) // 32 * 32
        return t

    xT = put("xT", [P, KB, S], F32)
    at_h = [at[0]]
    hhi = put("hhi", [P, KB, S], F32R)
    at_out = [at[0]]
    hlo = put("hlo", [P, KB, S], F32R)
    m_wo = put("m_wo", [P, KB, S], F32, at_h)
    outsb = put("outsb", [P, TB, D], F32, at_out)
    wraw = put("wraw", [P, 2, KB, 2 * P], F32)
    whi = put("whi", [P, 4, KB, P], F32R)
    wlo = put("wlo", [P, 4, KB, P], F32R)
    at_m, at_m2 = [at[0]], [at[0]]
    m = put("m", [P, KB, S], F32)
    xin = put("xin", [P, TB, D], F32, at_m)
    ohi = put("ohi", [P, KB, S], F32R, at_m2)
    olo = put("olo", [P, KB, S], F32R)
    arena = at[0]
    ahi = put("ahi", [P, 16, S], F32R)
    alo = put("alo", [P, 16, S], F32R)
    ca = [arena]
    y = put("y", [P, KB, S], F32, ca)
    upad = put("upad", [P, 2, PADW], F32, ca)
    uhi = put("uhi", [P, 2, PADW], F32R, ca)
    ulo = put("ulo", [P, 2, PADW], F32R, ca)
    acc1 = put("acc1", [P, S], F32, ca)
    dwhi = put("dwhi", [P, KB, PE_TAPS], F32R, ca)
    dwlo = put("dwlo", [P, KB, PE_TAPS], F32R, ca)
    cb = [ca[0]]
    diaghi = put("diaghi", [P, 2, PE_TAPS, P], F32R, ca)
    diaglo = put("diaglo", [P, 2, PE_TAPS, P], F32R, ca)
    vrows = put("vrows", [P, D], F32, cb)
    assert ca[0] <= at[0], (ca[0], at[0])
    aa = [arena]
    qhi = put("qhi", [P, S], F32R, aa)
    qlo = put("qlo", [P, S], F32R, aa)
    kzhi = put("kzhi", [P, 2, S], F32R, aa)
    kzlo = put("kzlo", [P, 2, S], F32R, aa)
    vhi = put("vhi", [P, TB, P], F32R, aa)
    vlo = put("vlo", [P, TB, P], F32R, aa)
    prob = put("prob", [P, 2, 10 * P], F32, aa)
    rhsF = put("rhsF", [P, S], F32R, aa)
    lhsB = put("lhsB", [P, S], F32, aa)
    lhsF = put("lhsF", [P, 2, S], F32R, aa)
    causal = put("causal", [P, S], F32, aa)
    ab, ac = [aa[0]], [aa[0]]
    pThi = put("pThi", [P, TB, S], F32R, aa)
    pTlo = put("pTlo", [P, TB, S], F32R, aa)
    wfhi = put("wfhi", [P, KB, P], F32R, ab)
    wflo = put("wflo", [P, KB, P], F32R, ab)
    Fhi = put("Fhi", [P, S], F32R, aa)
    fwork = put("fwork", [P, 7, S], F32, ac)
    FZ, FB, FABS, FEXP, FLN, FLOG, FCUM = range(7)
    assert aa[0] <= at[0], (aa[0], at[0])
    tmp = put("tmp", [P, 4, S], F32)
    sumsq = put("sumsq", [P, S], F32)
    rinv = put("rinv", [P, S], F32)
    vec = put("vec", [P, KB, V_ROWS], F32)
    ident = put("ident", [P, P], F32)
    ones = put("ones", [P, P], F32)
    wfraw = put("wfraw", [P, KB, HEADS], F32)
    onehot = put("onehot", [P, HEADS], F32)
    bf = put("bf", [P, 1], F32)
    eps = put("eps", [P, 2], F32)
    negmax = put("negmax", [P, 8], F32)
    den = put("den", [P, 8], F32)
    rden = put("rden", [P, 8], F32)
    rms = put("rms", [P, TB], F32)
    irms = put("irms", [P, TB], F32)
    assert base + at[0] <= nc.sbuf_usable_end - 256, (base + at[0], nc.sbuf_usable_end)

    psum = nc.alloc_psum_tensor("psum", [P, 8, 512], F32)
    STAT, SCORE, TRP, OUTP = 6, 4, (6, 3), 7

    sem_names = (
        "x_loaded0 x_loaded1 x_loaded2 x_loaded3 vec_loaded wf_loaded raw0 raw1 consts zeroed "
        "vt_done vec_ready xt_done xt_copied "
        "w_hi0 w_hi1 w_ready0 w_ready1 unit0 unit1 "
        "h_hi h_ready p_sq p_sum stat root irms_done spread bcast rinv_done "
        "m_done m_sq m_sum m_zero t1_done x_done "
        "glu_t glu_g glu_s glu_u u_hi u_ready dw_hi dw_lo diag conv_done tap acc y_done y_sum y_zero "
        "mean c_sub c_sq c_sum c_nrm c_silu c_hi c_ready "
        "up_evac up_sq up_hi a_ready dn_evac "
        "wf_zero wf_hi wf_ready f_done f_z f_b f_abs f_exp f_ln f_log f_cum f_hi f_lo f_rows f_base f_ready sel "
        "pr_evac q_hi q_ready k_hi k_ready vtr v_hi v_ready "
        "sc_done sc_seen sc_evac ex_done rc_done p_ready t_done p_hi pt_ready pv_done o_hi o_ready "
        "out_tr out_copied stored"
    ).split()
    s = {n: nc.alloc_semaphore(n) for n in sem_names}
    raw = (s["raw0"], s["raw1"])
    w_hi = (s["w_hi0"], s["w_hi1"])
    w_ready = (s["w_ready0"], s["w_ready1"])
    unit = (s["unit0"], s["unit1"])

    def flat(ap):
        return ap.rearrange("p a b -> p (a b)")

    def vcol(row, k):
        if isinstance(k, int):
            return vec[:, k, row:row + 1]
        return flat(vec[:, ds(k, 1), row:row + 1])

    def blk(t, k):
        if isinstance(k, int):
            return t[:, k, :]
        return flat(t[:, ds(k, 1), :])

    def probs(hh, j):
        o = P * (j * (j + 1) // 2)
        return prob[:, hh, o:o + P * (j + 1)]

    def mbuf(b):
        return m_wo if b == 2 else m

    with nc.Block() as block:

        @block.sync
        def _(sp):
            def load(n, r, parts):
                if not (isinstance(n, int) and n == 0):
                    sp.wait_ge(w_ready[r], 2 * n)
                for dst, src in parts:
                    sp.dma_start(dst, src).then_inc(raw[r], 16)

            def by_rows(w, r, col):
                wr = w.rearrange("(k p) f -> p k f", p=P)
                c = col if isinstance(col, int) else None
                sl = slice(c, c + 2 * P) if c is not None else ds(col, 2 * P)
                return [(wraw[:, r, 4 * k:4 * k + 4, :], wr[:, 4 * k:4 * k + 4, sl]) for k in range(2)]

            def by_cols(w, r, cols):
                wr = w.rearrange("(k p) f -> p k f", p=P)
                return [(wraw[:, r, :, P * c:P * c + P], wr[:, :, ds(cols[c], P)]) for c in range(2)]

            xr = x[0].rearrange("(q p) d -> p q d", p=P)
            for c in range(4):
                cols = slice(c * 2 * P, (c + 1) * 2 * P)
                sp.dma_start(xin[:, :, cols], xr[:, :, cols]).then_inc(s[f"x_loaded{c}"], 16)
            rows = [(V_MIX_PRE, 2, g_mix_pre), (V_MIX_POST, 2, g_mix_post), (V_FFN_PRE, 2, g_ffn_pre),
                    (V_FFN_POST, 2, g_ffn_post),
                    (V_PW1B, 2, conv_pw1_b.rearrange("a (b d) -> (a b) d", b=2)), (V_DWB, 1, conv_dw_b),
                    (V_LNG, 1, conv_ln_g), (V_LNB, 1, conv_ln_b), (V_PW2B, 1, conv_pw2_b),
                    (V_DW, W, conv_dw_w[0])]
            for row, n, src in rows:
                sp.dma_start(vrows[row:row + n, :], src).then_inc(s["vec_loaded"], 16)
            for n in range(1):
                for r in range(2):
                    load(n, r, by_cols(conv_pw1_w[0], r, [(2 * n + r) * P, D + (2 * n + r) * P]))
            sp.wait_ge(s["zeroed"], 1)
            for g in range(4):
                sp.dma_start(bf[32 * g:32 * g + HEADS, :],
                             attn_b_f.rearrange("a h -> h a")).then_inc(s["wf_loaded"], 16)
            sp.dma_start(wfraw[:, :, :],
                         attn_w_in[0].rearrange("(k p) f -> p k f", p=P)[:, :, 3 * D:3 * D + HEADS]
                         ).then_inc(s["wf_loaded"], 16)
            with sp.Fori(1, 4) as i:
                for r in range(2):
                    load(N_PW1 + i, r, by_cols(conv_pw1_w[0], r, [i * 256 + r * P, i * 256 + (D + r * P)]))
            for i in range(2):
                for r in range(2):
                    load(N_PW2 + i, r, by_rows(conv_pw2_w[0], r, (2 * i + r) * 2 * P))

            def mlp_loads(l, n0):
                for half in range(2):
                    with sp.Fori(0, 4) as i:
                        for r in range(2):
                            load(n0 + 8 * half + i, r,
                                 by_rows(mlp_w_up[l], r, i * 512 + (half * 2048 + r * 256)))
                    with sp.Fori(0, 4) as i:
                        for r in range(2):
                            rows_ = mlp_w_down[l, half * 2048 + r * D:half * 2048 + (r + 1) * D, :]
                            load(n0 + 8 * half + 4 + i, r, by_rows(rows_, r, i * 256))

            mlp_loads(0, N_MLP0)
            wv = attn_w_in[0].rearrange("(k p) f -> p k f", p=P)
            with sp.Fori(0, PAIRS) as i:
                load(N_ATT + i, 0, by_cols(attn_w_in[0], 0, [i * P, i * P + D]))
                load(N_ATT + i, 1, [(wraw[:, 1, 4 * k:4 * k + 4, 0:P],
                                     wv[:, 4 * k:4 * k + 4, ds(i * P + 2 * D, P)]) for k in range(2)])
            for i in range(2):
                for r in range(2):
                    load(N_WO + i, r, by_rows(attn_w_o[0], r, (2 * i + r) * 2 * P))
            mlp_loads(1, N_MLP1)
            od = out[0].rearrange("(q p) d -> p q d", p=P)
            for k in range(0, KB, 2):
                sp.wait_ge(s["out_copied"], k + 2)
                sp.dma_start(od[:, :, k * P:(k + 2) * P],
                             outsb[:, :, k * P:(k + 2) * P]).then_inc(s["stored"], 16)
            sp.wait_ge(s["stored"], 16 * (KB // 2))

        @block.gpsimd
        def _(pool):
            g = nc.gpsimd
            g.memset(bf[:, :], 0.0).then_inc(s["zeroed"], 1)
            g.memset(ident[:, :], 0.0).then_inc(s["consts"], 1)
            g.memset(ones[:, :], 1.0).then_inc(s["consts"], 1)
            g.memset(eps[:, 0:1], RMS_EPS).then_inc(s["consts"], 1)
            g.memset(eps[:, 1:2], LN_EPS).then_inc(s["consts"], 1)
            pool.wait_ge(s["consts"], 1)
            g.affine_select(out=ident[:, :], in_=ident[:, :], compare_op=ALU.not_equal, fill=1.0, base=0,
                            pattern=[[-1, P]], channel_multiplier=1).then_inc(s["consts"], 1)
            g.memset(upad[:, :, :], 0.0).then_inc(s["consts"], 1)
            g.memset(onehot[:, :], 0.0).then_inc(s["sel"], 1)
            for q in range(4):
                pool.wait_ge(s["sel"], q + 1)
                g.affine_select(out=onehot[:, :], in_=onehot[:, :], compare_op=ALU.not_equal, fill=1.0,
                                base=-32 * q, pattern=[[-1, HEADS]],
                                channel_multiplier=1).then_inc(s["sel"], 1)
            def y_total(j):
                pool.wait_ge(s["y_done"], j + 1)
                pool.wait_ge(s["y_sum"], j + 1)
                yb = blk(y, j)
                g.tensor_tensor(sumsq[:, :], sumsq[:, :], yb, ALU.add).then_inc(s["y_sum"], 1)

            pool.wait_ge(s["rinv_done"], 1)
            g.memset(sumsq[:, :], 0.0).then_inc(s["y_sum"], 1)
            with pool.Fori(0, KB) as i:
                y_total(i)

            pool.wait_ge(unit[1], 2 * (N_MLP0 + 15) + 4)
            g.memset(wfhi[:, :, :].bitcast(F32), 0.0).then_inc(s["wf_zero"], 1)
            g.memset(wflo[:, :, :].bitcast(F32), 0.0).then_inc(s["wf_zero"], 1)
            pool.wait_ge(s["wf_loaded"], 80)
            pool.wait_ge(s["wf_zero"], 2)
            wsrc = wfraw[:, :, :]
            for q in range(4):
                g.tensor_copy(wfhi[:, :, 32 * q:32 * q + HEADS], wsrc).then_inc(s["wf_hi"], 1)
                pool.wait_ge(s["wf_hi"], q + 1)
                g.tensor_tensor(wflo[:, :, 32 * q:32 * q + HEADS], wsrc,
                                wfhi[:, :, 32 * q:32 * q + HEADS].bitcast(F32),
                                ALU.subtract).then_inc(s["wf_ready"], 1)
            g.memset(kzhi[:, :, :].bitcast(F32), 0.0).then_inc(s["f_base"], 1)
            g.memset(kzlo[:, :, :].bitcast(F32), 0.0).then_inc(s["f_base"], 1)
            g.memset(rhsF[:, :].bitcast(F32), 1.0).then_inc(s["f_base"], 1)
            g.memset(lhsB[:, :], 1.0).then_inc(s["f_base"], 1)
            g.memset(causal[:, :], 0.0).then_inc(s["f_base"], 1)
            pool.wait_ge(s["f_base"], 5)
            g.affine_select(out=causal[:, S - P:S], in_=causal[:, S - P:S], compare_op=ALU.is_ge,
                            fill=MASK, base=0, pattern=[[-1, P]],
                            channel_multiplier=1).then_inc(s["f_base"], 1)
            pool.wait_ge(s["f_rows"], 4)
            def head_rows(h, hh):
                oh = onehot[:, h:h + 1] if isinstance(h, int) else onehot[:, ds(h, 1)]
                g.tensor_tensor(lhsF[:, hh, :], lhsB[:, :], oh.broadcast_to([P, S]),
                                ALU.mult).then_inc(s["f_ready"], 1)
            pool.wait_ge(s["sel"], 5)
            for hh in range(2):
                head_rows(hh, hh)
            with pool.Fori(1, PAIRS) as p:
                for hh in range(2):
                    pool.wait_ge(s["sc_done"], 8 * p + (4 * hh - 4))
                    head_rows(2 * p + hh, hh)

        @block.tensor
        def _(pe):
            pe.sem_inc(unit[0], 2)
            pe.sem_inc(unit[1], 2)
            pe.sem_inc(s["t_done"], 8)
            pe.sem_inc(s["pv_done"], 1)

            def product(bank, u, kb, xhi, xlo, start, stop, cols=None):
                o = psum[:, bank, :]
                pe.matmul(o, whi[:, u, kb, :], xhi, start=start, stop=False)
                pe.matmul(o, whi[:, u, kb, :], xlo, start=False, stop=False)
                return pe.matmul(o, wlo[:, u, kb, :], xhi, start=False, stop=stop)

            def weights(n, u):
                pe.wait_ge(w_ready[u // 2], 2 * n + (1 + u % 2))

            def first_step(n, ready, count):
                for u in range(4):
                    weights(n, u)
                for kb in range(KB - 2):
                    pe.wait_ge(ready, count + kb + 1)
                    for u in range(4):
                        product(u, u, kb, hhi[:, kb, :], hlo[:, kb, :], kb == 0, False)
                pe.wait_ge(ready, count + KB)
                for u in range(4):
                    for kb in (KB - 2, KB - 1):
                        mm = product(u, u, kb, hhi[:, kb, :], hlo[:, kb, :], False, kb == KB - 1)
                    mm.then_inc(unit[u // 2], 1)

            def whole_unit(n, u, xh=hhi, xl=hlo):
                weights(n, u)
                for kb in range(KB):
                    mm = product(u, u, kb, xh[:, kb, :], xl[:, kb, :], kb == 0, kb == KB - 1)
                mm.then_inc(unit[u // 2], 1)

            def columns(src, first, last):
                for q in range(TB):
                    mm = pe.matmul(psum[:, STAT, q:q + 1], src[:, q * P:(q + 1) * P], ones[:, 0:1],
                                   start=first and q == 0, stop=last, skip_group_check=True)
                return mm

            def broadcast(idx):
                pe.wait_ge(s["spread"], idx)
                pe.matmul(psum[:, STAT, :], ones[:, :], tmp[:, 0, :], start=True,
                          stop=True).then_inc(s["bcast"], 1)

            def pre_stat(v):
                pe.wait_ge(s["p_sum"], KB * (v + 1))
                columns(sumsq, True, True).then_inc(s["stat"], 1)
                broadcast(NTH[ST_PRE[v]])

            def post_stat(b):
                pe.wait_ge(s["m_sum"], 7 * b + 9)
                columns(sumsq, True, False)
                pe.wait_ge(s["m_sq"], KB * (b + 1))
                columns(tmp[:, 3, :], False, True).then_inc(s["stat"], 1)
                broadcast(NTH[ST_POST[b]])

            pe.wait_ge(s["consts"], 6)
            pe.wait_ge(s["vec_loaded"], 160)
            for k in range(KB):
                t = pe.transpose(psum[:, 7, k * V_ROWS:(k + 1) * V_ROWS], vrows[0:V_ROWS, k * P:(k + 1) * P],
                                 ident[0:V_ROWS, 0:V_ROWS])
            t.then_inc(s["vt_done"], 1)
            for k in range(KB):
                pe.wait_ge(s[f"x_loaded{k // 2}"], 16)
                if k >= 2:
                    pe.wait_ge(s["xt_copied"], k - 1)
                for q in range(TB):
                    t = pe.transpose(psum[:, 4 + k % 2, q * P:(q + 1) * P], xin[:, q, k * P:(k + 1) * P],
                                     ident[:, :])
                t.then_inc(s["xt_done"], 1)

            def conv(j, r):
                pe.wait_ge(s["u_ready"], j + 1)
                pe.wait_ge(s["diag"], j + 1)
                if not (isinstance(j, int) and j < 2):
                    pe.wait_ge(s["y_done"], j - 1)
                o = psum[:, 4 + r, :]
                for k in range(PE_TAPS):
                    t = DVE_TAPS + k
                    dh, dl = diaghi[:, r, k, :], diaglo[:, r, k, :]
                    xh, xl = uhi[:, r, t:t + S], ulo[:, r, t:t + S]
                    pe.matmul(o, dh, xh, start=k == 0, stop=False)
                    pe.matmul(o, dh, xl, start=False, stop=False)
                    mm = pe.matmul(o, dl, xh, start=False, stop=k == PE_TAPS - 1)
                mm.then_inc(s["conv_done"], 1)

            first_step(N_PW1, s["h_ready"], 0)
            pre_stat(0)
            conv(0, 0)
            with pe.Fori(1, 4) as i:
                for r in range(2):
                    pe.wait_ge(s["glu_u"], 2 * i + (r - 1))
                    for u in (2 * r, 2 * r + 1):
                        whole_unit(N_PW1 + i, u)
                    conv(2 * i + (r - 1), 1 - r)
            conv(7, 1)
            pe.wait_ge(s["y_sum"], KB + 1)
            pe.matmul(psum[:, STAT, :], ones[:, :], sumsq[:, :], start=True,
                      stop=True).then_inc(s["mean"], 1)
            for k in range(KB):
                pe.wait_ge(s["c_sq"], k + 1)
                sq = tmp[:, 2 + k % 2, :]
                for q in range(TB):
                    mm = pe.matmul(psum[:, 7, q:q + 1], sq[:, q * P:(q + 1) * P], ones[:, 0:1],
                                   start=k == 0 and q == 0, stop=k == KB - 1, skip_group_check=True)
                mm.then_inc(s["c_sum"], 1)
            broadcast(NTH[ST_VAR])

            first_step(N_PW2, s["c_ready"], 0)
            for u in range(4):
                pe.wait_ge(s["m_done"], u + 3)
                whole_unit(N_PW2 + 1, u)
            post_stat(0)

            def mlp(l, n0, v, b):
                for half in range(2):
                    q = 2 * l + half
                    if half == 0:
                        first_step(n0, s["h_ready"], KB * v)
                        pre_stat(v)
                        i0 = 1
                    else:
                        i0 = 0
                    with pe.Fori(i0, 4) as i:
                        for u in range(4):
                            if q > 0 or i0 == 1:
                                pe.wait_ge(s["up_evac"], 4 * i + (16 * q - 4 + u + 1))
                            whole_unit(n0 + 8 * half + i, u)
                    if half == 1:
                        pe.wait_ge(s["dn_evac"], 8 * (l + 1) + 2)
                    with pe.Fori(0, 4) as i:
                        n = n0 + 8 * half + 4 + i
                        for u in range(4):
                            kg, f = u // 2, u % 2
                            weights(n, u)
                            pe.wait_ge(s["a_ready"], 16 * q + 8 * (kg + 1))
                            if kg == 0 and half == 0:
                                pe.wait_ge(s["dn_evac"], 2 * i + (8 * l + f + 1))
                            if kg == 0 and half == 1:
                                pe.wait_ge(s["m_done"], 2 * i + (8 * b + f + 1))
                            for kb in range(KB):
                                a = 8 * kg + kb
                                mm = product(4 + f, u, kb, ahi[:, a, :], alo[:, a, :],
                                             kg == 0 and kb == 0, kg == 1 and kb == KB - 1)
                            mm.then_inc(unit[u // 2], 1)
                post_stat(b)

            mlp(0, N_MLP0, 1, 1)

            for u in range(2):
                weights(N_ATT, u)
            pe.wait_ge(w_ready[1], 2 * N_ATT + 2)
            pe.wait_ge(s["wf_ready"], 4)

            def gate_product(kb):
                o = psum[:, 3, :]
                pe.matmul(o, wfhi[:, kb, :], hhi[:, kb, :], start=kb == 0, stop=False)
                pe.matmul(o, wfhi[:, kb, :], hlo[:, kb, :], start=False, stop=False)
                return pe.matmul(o, wflo[:, kb, :], hhi[:, kb, :], start=False, stop=kb == KB - 1)

            for kb in range(KB - 2):
                pe.wait_ge(s["h_ready"], 2 * KB + kb + 1)
                gate_product(kb)
                for u in range(3):
                    product(u, u, kb, hhi[:, kb, :], hlo[:, kb, :], kb == 0, False)
            pe.wait_ge(s["h_ready"], 3 * KB)
            for kb in (KB - 2, KB - 1):
                mm = gate_product(kb)
            mm.then_inc(s["f_done"], 1)
            pre_stat(2)
            for u in range(3):
                for kb in (KB - 2, KB - 1):
                    mm = product(u, u, kb, hhi[:, kb, :], hlo[:, kb, :], False, kb == KB - 1)
                mm.then_inc(unit[u // 2], 2 if u == 2 else 1)

            def attention(p, project, fill=None):
                for what, i in SEQ:
                    hh, j = i // 4, i % 4
                    if what == "S":
                        if i == 0:
                            pe.wait_ge(s["q_ready"], p + 1)
                            pe.wait_ge(s["k_ready"], 2 * p + 2)
                        if j == 0:
                            pe.wait_ge(s["f_ready"], 2 * p + (hh + 1))
                        pe.wait_ge(s["sc_evac"], 8 * p + (i + 1))
                        n = P * (j + 1)
                        o = psum[:, SCORE + i % 2, 0:n]
                        qb = slice(j * P, (j + 1) * P)
                        pe.matmul(o, lhsF[:, hh, qb], rhsF[:, 0:n], start=True, stop=False)
                        pe.matmul(o, qhi[:, qb], kzhi[:, hh, 0:n], start=False, stop=False)
                        pe.matmul(o, qhi[:, qb], kzlo[:, hh, 0:n], start=False, stop=False)
                        pe.matmul(o, qlo[:, qb], kzhi[:, hh, 0:n], start=False,
                                  stop=True).then_inc(s["sc_done"], 1)
                    if what == "V":
                        pe.wait_ge(s["pr_evac"], 3 * p + 6)
                        pe.wait_ge(s["pt_ready"], 8 * p + 2)
                        for q in range(TB):
                            t = pe.transpose(psum[:, 3, q * P:(q + 1) * P], tmp[:, 2, q * P:(q + 1) * P],
                                             ident[:, :])
                        t.then_inc(s["vtr"], 1)
                    if what == "P" and fill:
                        for kb, u in fill[i]:
                            product(u, u, kb, ohi[:, kb, :], olo[:, kb, :], kb == 0, False)
                    if what == "P" and project:
                        u, part = i // 4, i % 4
                        n = N_ATT + 1 + p
                        if part == 0:
                            weights(n, u) if u < 2 else pe.wait_ge(w_ready[1], 2 * n + 2)
                            pe.wait_ge(s["pr_evac"], 3 * p + (3 + u + 1))
                        for kb in (2 * part, 2 * part + 1):
                            mm = product(u, u, kb, hhi[:, kb, :], hlo[:, kb, :], kb == 0, kb == KB - 1)
                        if part == 3:
                            mm.then_inc(unit[u // 2], 2 if u == 2 else 1)
                    if what == "T":
                        pe.wait_ge(s["p_ready"], 8 * p + (i + 1))
                        pe.wait_ge(s["pt_ready"], 8 * p + (i + 1))
                        if i == 1:
                            pe.wait_ge(s["v_ready"], p + 1)
                        pr = probs(hh, j)
                        for kb in range(j + 1):
                            t = pe.transpose(psum[:, TRP[i % 2], kb * P:(kb + 1) * P], pr[:, kb * P:(kb + 1) * P],
                                             ident[:, :])
                        t.then_inc(s["t_done"], 1)
                    if what == "O":
                        pe.wait_ge(s["v_ready"], p + 1)
                        pe.wait_ge(s["pt_ready"], 8 * p + (4 * i + 6))
                        pe.wait_ge(s["o_ready"], 2 * p + (i + 1))
                        for kb in range(TB):
                            o = psum[:, OUTP, kb * P:S]
                            ph, pl = pThi[:, kb, kb * P:S], pTlo[:, kb, kb * P:S]
                            pe.matmul(o, vhi[:, kb, :], ph, start=kb == 0, stop=False)
                            pe.matmul(o, vhi[:, kb, :], pl, start=False, stop=False)
                            mm = pe.matmul(o, vlo[:, kb, :], ph, start=False, stop=kb == TB - 1)
                        mm.then_inc(s["pv_done"], 1)

            with pe.Fori(0, PAIRS - 2) as p:
                attention(p, True)
            attention(PAIRS - 2, True)
            fill = [(kb, u) for kb in range(KB - 1) for u in range(3)]
            pe.wait_ge(s["o_ready"], 2 * (PAIRS - 1) + 1)
            pe.wait_ge(s["pr_evac"], 3 * PAIRS + 3)
            for u in range(3):
                weights(N_WO, u)
            attention(PAIRS - 1, False, [fill[2 * i:2 * i + 2] for i in range(PARTS_OF_P)])

            pe.wait_ge(s["o_ready"], 2 * PAIRS + 1)
            for u in range(3):
                product(u, u, KB - 1, ohi[:, KB - 1, :], olo[:, KB - 1, :], False,
                        True).then_inc(unit[u // 2], 1)
            whole_unit(N_WO, 3, ohi, olo)
            for u in range(4):
                pe.wait_ge(s["m_done"], 16 + u + 3)
                whole_unit(N_WO + 1, u, ohi, olo)
            post_stat(2)
            mlp(1, N_MLP1, 3, 3)
            for k in range(KB):
                pe.wait_ge(s["x_done"], 3 * KB + k + 1)
                if k >= 2:
                    pe.wait_ge(s["out_copied"], k - 1)
                for q in range(TB):
                    t = pe.transpose(psum[:, k % 2, q * P:(q + 1) * P], xT[:, k, q * P:(q + 1) * P],
                                     ident[:, :])
                t.then_inc(s["out_tr"], 1)

        @block.scalar
        def _(act):
            a = nc.scalar

            def split_hi(n, u, single=False):
                r, c = u // 2, u % 2
                act.wait_ge(raw[r], 32 * n + 32)
                act.wait_ge(unit[r], 2 * n + (2 if single else 1 + c))
                a.activation(whi[:, u, :, :], wraw[:, r, :, c * P:(c + 1) * P],
                             ACT.Copy).then_inc(w_hi[r], 2 if single else 1)

            def done(n, u):
                act.wait_ge(unit[u // 2], 2 * n + (3 + u % 2))

            def square(src, k, sem_in, count, sem_free, free, sem_out):
                act.wait_ge(sem_in, count)
                if free is not None:
                    act.wait_ge(sem_free, free)
                a.activation(tmp[:, 2 + k % 2, :], src, ACT.Square).then_inc(sem_out, 1)

            def pre_norm(v, row, x_sem, x_count, also=None):
                for k in range(KB):
                    act.wait_ge(x_sem, x_count + k + 1)
                    a.activation(hhi[:, k, :], xT[:, k, :], ACT.Identity,
                                 scale=vcol(row, k)).then_inc(s["h_hi"], 1)
                    square(xT[:, k, :], k, x_sem, x_count + k + 1, s["p_sum"],
                           KB * v + k - 1 if KB * v + k > 1 else None, s["p_sq"])
                    if also:
                        also(k)

            def root(idx, e=0, bank=STAT):
                if idx == ST_VAR:
                    act.wait_ge(s["c_sum"], KB)
                else:
                    act.wait_ge(s["stat"], NTH[idx] - (NTH[idx] > NTH[ST_VAR]))
                a.activation(rms[:, :], psum[:, bank, 0:TB], ACT.Sqrt, scale=1.0 / D,
                             bias=eps[:, e:e + 1]).then_inc(s["root"], 1)

            def keep_row(idx):
                act.wait_ge(s["bcast"], NTH[idx])
                a.activation(rinv[:, :], psum[:, STAT, :], ACT.Copy).then_inc(s["rinv_done"], 1)

            act.wait_ge(s["vec_ready"], 1)
            a.activation(dwhi[:, :, :], vec[:, :, V_DW + DVE_TAPS:V_DW + W],
                         ACT.Copy).then_inc(s["dw_hi"], 1)
            pre_norm(0, V_MIX_PRE, s["xt_copied"], 0, lambda k: k < 4 and split_hi(0, k))
            root(ST_PRE[0])
            keep_row(ST_PRE[0])

            def diagonals(j, r):
                for k in range(PE_TAPS):
                    for dst, src in ((diaghi, dwhi), (diaglo, dwlo)):
                        col = src[:, j, k:k + 1] if isinstance(j, int) else flat(src[:, ds(j, 1), k:k + 1])
                        i_ = a.activation(dst[:, r, k, :], ident[:, :], ACT.Identity,
                                          scale=col.bitcast(F32))
                i_.then_inc(s["diag"], 1)

            def conv_step(n, last=False):
                for r in range(2):
                    j = 2 * n + r
                    act.wait_ge(s["glu_g"], j + 1)
                    a.activation(tmp[:, 1, :], tmp[:, 0, :], ACT.Sigmoid, bias=vcol(V_PW1B + 1, j)
                                 ).then_inc(s["glu_s"], 1)
                    act.wait_ge(s["glu_u"], j + 1)
                    if not (isinstance(j, int) and j < 2):
                        act.wait_ge(s["conv_done"], j - 1)
                    a.activation(uhi[:, r, :], upad[:, r, :], ACT.Copy).then_inc(s["u_hi"], 1)
                    for c in range(2):
                        split_hi(n + 1, 2 * r + c)
                    if not (last and r == 1):
                        if not (isinstance(j, int) and j < 1):
                            act.wait_ge(s["conv_done"], j)
                        diagonals(j + 1, 1 - r)
            act.wait_ge(s["dw_lo"], 1)
            diagonals(0, 0)
            conv_step(0)
            with act.Fori(1, 3) as i:
                conv_step(i)
            conv_step(3, last=True)
            for k in range(KB):
                square(y[:, k, :], k, s["c_sub"], k + 1, s["c_sum"], k - 1 if k > 1 else None, s["c_sq"])
            root(ST_VAR, 1, 7)
            for k in range(KB):
                act.wait_ge(s["c_nrm"], k + 1)
                if k >= 2:
                    act.wait_ge(s["c_ready"], k - 1)
                a.activation(tmp[:, k % 2, :], y[:, k, :], ACT.Silu, scale=vcol(V_LNG, k),
                             bias=vcol(V_LNB, k)).then_inc(s["c_silu"], 1)
                act.wait_ge(s["c_silu"], k + 1)
                a.activation(hhi[:, k, :], tmp[:, k % 2, :], ACT.Copy).then_inc(s["c_hi"], 1)

            def mixer_out(n0, b, dst, bias_row):
                for i in range(2):
                    for u in range(4):
                        k = 4 * i + u
                        done(n0 + i, u)
                        if bias_row is None:
                            e = a.activation(dst[:, k, :], psum[:, u, :], ACT.Copy)
                        else:
                            e = a.activation(dst[:, k, :], psum[:, u, :], ACT.Identity,
                                             bias=vcol(bias_row, k))
                        e.then_inc(s["m_done"], 1)
                        square(dst[:, k, :], k, s["m_done"], KB * b + k + 3, s["m_sum"],
                               7 * b + k + 1, s["m_sq"])
                        if k < KB - 1:
                            split_hi(n0 + i + 1, u)
                root(ST_POST[b])
                split_hi(n0 + 2, 3)

            mixer_out(N_PW2, 0, m, V_PW2B)

            def mlp(l, n0, b, last):
                v = 1 if l == 0 else 3
                pre_norm(v, V_FFN_PRE + l, s["x_done"], KB * (b - 1))
                root(ST_PRE[v])
                keep_row(ST_PRE[v])
                for half in range(2):
                    q = 2 * l + half
                    def up(i):
                        for u in range(4):
                            act.wait_ge(s["up_sq"], 4 * i + (16 * q + u + 1))
                            a.activation(blk(ahi, 4 * i + u), tmp[:, 2 + u % 2, :],
                                         ACT.Copy).then_inc(s["up_hi"], 1)
                            split_hi(n0 + 8 * half + i + 1, u)
                    with act.Fori(0, 4) as i:
                        up(i)
                    nd = n0 + 8 * half + 4
                    def down(i):
                        for u in range(4):
                            if u >= 2:
                                f = u - 2
                                if half == 0:
                                    done(nd + i, u)
                                    a.activation(blk(m, 2 * i + f), psum[:, 4 + f, :],
                                                 ACT.Copy).then_inc(s["dn_evac"], 1)
                                else:
                                    square(blk(m, 2 * i + f), f, s["m_done"], 2 * i + (KB * b + f + 3),
                                           s["m_sum"], 2 * i + (7 * b + f + 1), s["m_sq"])
                            split_hi(nd + i + 1, u)
                    if half == 0:
                        with act.Fori(0, 4) as i:
                            down(i)
                        continue
                    with act.Fori(0, 3) as i:
                        down(i)
                    nx = nd + 4
                    for u in range(0 if last else 2):
                        split_hi(nx, u)
                    for f in range(2):
                        square(m[:, 6 + f, :], f, s["m_done"], 6 + KB * b + f + 3,
                               s["m_sum"], 6 + 7 * b + f + 1, s["m_sq"])
                    root(ST_POST[b])
                    if not last:
                        split_hi_att(nx, 2)

            def split_hi_att(n, u):
                split_hi(n, u, single=u == 2)

            a.sem_inc(s["dn_evac"], 2)
            mlp(0, N_MLP0, 1, False)
            pre_norm(2, V_MIX_PRE + 1, s["x_done"], KB)
            root(ST_PRE[2])
            keep_row(ST_PRE[2])

            def q_hi(p):
                act.wait_ge(s["pr_evac"], 3 * p + 4)
                if not (isinstance(p, int) and p == 0):
                    act.wait_ge(s["sc_done"], 8 * p)
                a.activation(qhi[:, :], tmp[:, 0, :], ACT.Copy).then_inc(s["q_hi"], 1)

            def k_hi(p):
                act.wait_ge(s["pr_evac"], 3 * p + 5)
                for hh in range(2):
                    rows = slice(HD * hh, HD * hh + HD)
                    a.activation(kzhi[rows, hh, :], tmp[rows, 1, :], ACT.Copy).then_inc(s["k_hi"], 1)

            act.wait_ge(s["f_z"], 1)
            act.wait_ge(s["wf_loaded"], 80)
            a.activation(fwork[:, FABS, :], fwork[:, FZ, :], ACT.Abs, bias=bf[:, 0:1]).then_inc(s["f_abs"], 1)
            act.wait_ge(s["f_abs"], 1)
            a.activation(fwork[:, FEXP, :], fwork[:, FABS, :], ACT.Exp, scale=-1.0).then_inc(s["f_exp"], 1)
            act.wait_ge(s["f_exp"], 1)
            a.activation(fwork[:, FLN, :], fwork[:, FEXP, :], ACT.Ln, bias=1.0).then_inc(s["f_ln"], 1)
            q_hi(0)
            act.wait_ge(s["f_base"], 6)
            k_hi(0)
            act.wait_ge(s["f_cum"], 1)
            a.activation(Fhi[:, :], fwork[:, FCUM, :], ACT.Copy).then_inc(s["f_hi"], 1)
            act.wait_ge(s["f_hi"], 1)
            a.activation(rhsF[0:HEADS, :], Fhi[0:HEADS, :].bitcast(F32), ACT.Copy).then_inc(s["f_rows"], 1)
            a.activation(lhsB[64:64 + HEADS, :], Fhi[64:64 + HEADS, :].bitcast(F32), ACT.Copy,
                         scale=-1.0).then_inc(s["f_rows"], 1)
            for u in range(3):
                split_hi_att(N_ATT + 1, u)

            def attention(p, project, units):
                for what, i in SEQ:
                    hh, j = i // 4, i % 4
                    if what == "S":
                        act.wait_ge(s["sc_evac"], 8 * p + (i + 3))
                        pr = probs(hh, j)
                        a.activation(pr, pr, ACT.Exp, scale=-1.0, bias=negmax[:, i:i + 1],
                                     accum_out=den[:, i:i + 1]).then_inc(s["ex_done"], 1)
                    if what == "V":
                        act.wait_ge(s["vtr"], p + 1)
                        act.wait_ge(s["pv_done"], 2 * p + 1)
                        a.activation(flat(vhi[:, :, :]), psum[:, 3, :], ACT.Copy).then_inc(s["v_hi"], 1)
                    if what == "PARTS" and project:
                        (q_hi, k_hi)[i](p + 1)
                    if what == "SPLIT" and project:
                        n = N_ATT + 2 + p
                        if units == 3:
                            split_hi_att(n, i)
                        else:
                            for u in (i,) if i < 2 else (2, 3):
                                split_hi(n, u)
                    if what == "T":
                        act.wait_ge(s["t_done"], 8 * p + (i + 9))
                        if j == 0:
                            act.wait_ge(s["pv_done"], 2 * p + (hh + 1))
                        src = psum[:, TRP[i % 2], 0:(j + 1) * P].rearrange("p (a b) -> p a b", b=P)
                        a.activation(pThi[:, 0:j + 1, j * P:(j + 1) * P], src,
                                     ACT.Copy).then_inc(s["p_hi"], 1)
                    if what == "O":
                        act.wait_ge(s["pv_done"], 2 * p + (i + 2))
                        rows = slice(HD * i, HD * i + HD)
                        dst = ohi[rows, p, :] if isinstance(p, int) else flat(ohi[rows, ds(p, 1), :])
                        a.activation(dst, psum[rows, OUTP, :], ACT.Copy).then_inc(s["o_hi"], 1)

            with act.Fori(0, PAIRS - 2) as p:
                attention(p, True, 3)
            attention(PAIRS - 2, True, 4)
            attention(PAIRS - 1, False, 0)
            mixer_out(N_WO, 2, m_wo, None)
            mlp(1, N_MLP1, 3, True)

        @block.vector
        def _(dve):
            d = nc.vector

            def split_lo(n, u, single=False):
                r, c = u // 2, u % 2
                dve.wait_ge(w_hi[r], 2 * n + (2 if single else 1 + c))
                d.tensor_tensor(wlo[:, u, :, :], wraw[:, r, :, c * P:(c + 1) * P],
                                whi[:, u, :, :].bitcast(F32), ALU.subtract
                                ).then_inc(w_ready[r], 2 if single else 1)

            def done(n, u):
                dve.wait_ge(unit[u // 2], 2 * n + (3 + u % 2))

            def h_lo(v, row, k):
                dve.wait_ge(s["h_hi"], KB * v + k + 1)
                d.scalar_tensor_tensor(hlo[:, k, :], xT[:, k, :], vcol(row, k), hhi[:, k, :].bitcast(F32),
                                       ALU.mult, ALU.subtract).then_inc(s["h_ready"], 1)

            def add_square(k, sem_in, count, sem_out, prev):
                dve.wait_ge(sem_in, count)
                if k == 0:
                    d.tensor_copy(sumsq[:, :], tmp[:, 2 + k % 2, :]).then_inc(sem_out, 1)
                else:
                    dve.wait_ge(sem_out, prev)
                    d.tensor_tensor(sumsq[:, :], sumsq[:, :], tmp[:, 2 + k % 2, :],
                                    ALU.add).then_inc(sem_out, 1)

            def inverse(idx, free=None):
                dve.wait_ge(s["root"], NTH[idx])
                d.reciprocal(irms[:, :], rms[:, :]).then_inc(s["irms_done"], 1)
                dve.wait_ge(s["irms_done"], NTH[idx])
                idb = ident[:, :].rearrange("p (a c) -> p a c", a=1).broadcast_to([P, TB, P])
                col = irms[:, :].rearrange("p (a c) -> p a c", c=1).broadcast_to([P, TB, P])
                d.tensor_tensor(tmp[:, 0, :].rearrange("p (a c) -> p a c", c=P), idb, col,
                                ALU.mult).then_inc(s["spread"], 1)

            d.sem_inc(s["m_done"], 2)
            d.sem_inc(s["m_sum"], 2)
            d.sem_inc(s["sc_evac"], 2)
            d.sem_inc(s["pt_ready"], 2)
            d.sem_inc(s["o_ready"], 1)
            d.sem_inc(s["pr_evac"], 3)
            dve.wait_ge(s["vt_done"], 1)
            d.tensor_copy(flat(vec[:, :, :]), psum[:, 7, 0:KB * V_ROWS]).then_inc(s["vec_ready"], 1)
            for k in range(KB + 1):
                if k < KB:
                    dve.wait_ge(s["xt_done"], k + 1)
                    d.tensor_copy(xT[:, k, :], psum[:, 4 + k % 2, :]).then_inc(s["xt_copied"], 1)
                if k >= 1:
                    h_lo(0, V_MIX_PRE, k - 1)
                    add_square(k - 1, s["p_sq"], k, s["p_sum"], k - 1)
                if 1 <= k <= 4:
                    split_lo(0, k - 1)
            dve.wait_ge(s["dw_hi"], 1)
            d.tensor_tensor(dwlo[:, :, :], vec[:, :, V_DW + DVE_TAPS:V_DW + W], dwhi[:, :, :].bitcast(F32),
                            ALU.subtract).then_inc(s["dw_lo"], 1)
            inverse(ST_PRE[0])

            def tap(j, r, t):
                g = DVE_TAPS * j + t
                dst = blk(y, j) if t % 2 == 0 else acc1[:, :]
                src = upad[:, r, t:t + S]
                if t == 0:
                    i = d.tensor_scalar(dst, src, vcol(V_DW, j), vcol(V_DWB, j), ALU.mult, ALU.add)
                elif t == 1:
                    i = d.tensor_scalar(dst, src, vcol(V_DW + 1, j), None, ALU.mult)
                else:
                    dve.wait_ge(s["tap"], g - 1)
                    i = d.scalar_tensor_tensor(dst, src, vcol(V_DW + t, j), dst, ALU.mult, ALU.add)
                i.then_inc(s["tap"], 1)

            def conv_block(n, r):
                j = 2 * n + r
                if isinstance(j, int) and j == 0:
                    dve.wait_ge(s["rinv_done"], RINV_NTH[ST_PRE[0]])
                done(N_PW1 + n, 2 * r + 1)
                if not (isinstance(j, int) and j == 0):
                    dve.wait_ge(s["glu_u"], j)
                d.tensor_tensor(tmp[:, 0, :], psum[:, 2 * r + 1, :], rinv[:, :],
                                ALU.mult).then_inc(s["glu_g"], 1)
                d.tensor_tensor(tmp[:, 2, :], psum[:, 2 * r, :], rinv[:, :],
                                ALU.mult).then_inc(s["glu_t"], 1)
                dve.wait_ge(s["glu_t"], j + 1)
                dve.wait_ge(s["glu_s"], j + 1)
                if isinstance(j, int) and j < 2:
                    dve.wait_ge(s["consts"], 6)
                else:
                    dve.wait_ge(s["u_ready"], j - 1)
                d.scalar_tensor_tensor(upad[:, r, W - 1:W - 1 + S], tmp[:, 2, :], vcol(V_PW1B, j),
                                       tmp[:, 1, :], ALU.add, ALU.mult).then_inc(s["glu_u"], 1)
                dve.wait_ge(s["glu_u"], j + 1)
                tap(j, r, 0)
                if not (isinstance(j, int) and j == 0):
                    dve.wait_ge(s["y_done"], j)
                tap(j, r, 1)
                dve.wait_ge(s["u_hi"], j + 1)
                d.tensor_tensor(ulo[:, r, :], upad[:, r, :], uhi[:, r, :].bitcast(F32),
                                ALU.subtract).then_inc(s["u_ready"], 1)
                for t in range(2, DVE_TAPS):
                    tap(j, r, t)
                    if t == DVE_TAPS // 2:
                        split_lo(n + 1, 2 * r)
                split_lo(n + 1, 2 * r + 1)
                dve.wait_ge(s["tap"], DVE_TAPS * (j + 1))
                d.tensor_tensor(acc1[:, :], acc1[:, :], blk(y, j), ALU.add).then_inc(s["acc"], 1)
                dve.wait_ge(s["acc"], j + 1)
                dve.wait_ge(s["conv_done"], j + 1)
                d.tensor_tensor(blk(y, j), psum[:, 4 + r, :], acc1[:, :], ALU.add
                                ).then_inc(s["y_done"], 1)

            def conv_step(n):
                for r in range(2):
                    conv_block(n, r)
            conv_step(0)
            with dve.Fori(1, 4) as i:
                conv_step(i)
            dve.wait_ge(s["mean"], 1)
            for k in range(KB):
                d.scalar_tensor_tensor(y[:, k, :], psum[:, STAT, :], -1.0 / D, y[:, k, :], ALU.mult,
                                       ALU.add).then_inc(s["c_sub"], 1)
            inverse(ST_VAR)
            dve.wait_ge(s["bcast"], NTH[ST_VAR])
            for k in range(KB + 1):
                if k < KB:
                    d.tensor_tensor(y[:, k, :], y[:, k, :], psum[:, STAT, :], ALU.mult
                                    ).then_inc(s["c_nrm"], 1)
                if k >= 1:
                    dve.wait_ge(s["c_hi"], k)
                    d.tensor_tensor(hlo[:, k - 1, :], tmp[:, (k - 1) % 2, :], hhi[:, k - 1, :].bitcast(F32),
                                    ALU.subtract).then_inc(s["c_ready"], 1)

            def mixer_out(n0, b):
                for i in range(2):
                    for u in range(4):
                        k = 4 * i + u
                        if k < KB - 1:
                            add_square(k, s["m_sq"], KB * b + k + 1, s["m_sum"], 7 * b + k + 2)
                            split_lo(n0 + i + 1, u)

            def boundary(b, row_post, v, row_pre):
                inverse(ST_POST[b])
                if b in (0, 2):
                    split_lo(N_MLP0 if b == 0 else N_MLP1, 3)
                dve.wait_ge(s["bcast"], NTH[ST_POST[b]])
                src = mbuf(b)
                for k in range(KB + 1):
                    c = KB * b + k
                    if k < KB:
                        if c >= 2:
                            dve.wait_ge(s["x_done"], c - 1)
                        d.scalar_tensor_tensor(tmp[:, k % 2, :], src[:, k, :], vcol(row_post, k),
                                               psum[:, STAT, :], ALU.mult, ALU.mult).then_inc(s["t1_done"], 1)
                        dve.wait_ge(s["t1_done"], c + 1)
                        d.tensor_tensor(xT[:, k, :], xT[:, k, :], tmp[:, k % 2, :],
                                        ALU.add).then_inc(s["x_done"], 1)
                    if k >= 1 and v is not None:
                        h_lo(v, row_pre, k - 1)
                        add_square(k - 1, s["p_sq"], KB * v + k, s["p_sum"], KB * v + k - 1)
                if v is not None:
                    inverse(ST_PRE[v])
                    dve.wait_ge(s["rinv_done"], RINV_NTH[ST_PRE[v]])

            mixer_out(N_PW2, 0)
            boundary(0, V_MIX_POST, 1, V_FFN_PRE)

            def mlp(l, n0, b, last):
                for half in range(2):
                    q = 2 * l + half
                    def a_lo(i, u):
                        dve.wait_ge(s["up_hi"], 4 * i + (16 * q + u + 1))
                        d.tensor_tensor(blk(alo, 4 * i + u), tmp[:, 2 + u % 2, :],
                                        blk(ahi, 4 * i + u).bitcast(F32),
                                        ALU.subtract).then_inc(s["a_ready"], 1)
                    def up(i, peeled):
                        n = n0 + 8 * half + i
                        for u in range(4):
                            c = 4 * i + (16 * q + u)
                            done(n, u)
                            if not (q == 0 and peeled and u == 0):
                                dve.wait_ge(s["up_sq"], c)
                            d.tensor_tensor(tmp[:, 0, :], psum[:, u, :], rinv[:, :],
                                            ALU.mult).then_inc(s["up_evac"], 1)
                            dve.wait_ge(s["up_evac"], c + 1)
                            if not (q == 0 and peeled and u < 2):
                                dve.wait_ge(s["a_ready"], c - 1)
                            d.scalar_tensor_tensor(tmp[:, 2 + u % 2, :], tmp[:, 0, :], 0.0, tmp[:, 0, :],
                                                   ALU.max, ALU.mult).then_inc(s["up_sq"], 1)
                            if u >= 1:
                                a_lo(i, u - 1)
                            split_lo(n + 1, u)
                        a_lo(i, 3)
                    up(0, True)
                    with dve.Fori(1, 4) as i:
                        up(i, False)
                    nd = n0 + 8 * half + 4
                    if half == 0:
                        with dve.Fori(0, 4) as i:
                            for u in range(4):
                                split_lo(nd + i + 1, u)
                        continue
                    d.memset(sumsq[:, :], 0.0).then_inc(s["m_zero"], 1)
                    dve.wait_ge(s["m_zero"], l + 1)
                    def add_sq(i, f):
                        dve.wait_ge(s["m_sq"], 2 * i + (KB * b + f + 1))
                        dve.wait_ge(s["m_sum"], 2 * i + (7 * b + f + 2))
                        d.tensor_tensor(sumsq[:, :], sumsq[:, :], tmp[:, 2 + f, :],
                                        ALU.add).then_inc(s["m_sum"], 1)
                    def down(i):
                        for u in range(4):
                            if u >= 2:
                                f = u - 2
                                done(nd + i, u)
                                mb = blk(m, 2 * i + f)
                                d.tensor_tensor(mb, psum[:, 4 + f, :], mb, ALU.add).then_inc(s["m_done"], 1)
                            if u == 3:
                                add_sq(i, 0)
                            split_lo(nd + i + 1, u)
                        add_sq(i, 1)
                    dve.wait_ge(s["dn_evac"], 8 * (l + 1) + 2)
                    with dve.Fori(0, 3) as i:
                        down(i)
                    nx = nd + 4
                    for u in range(0 if last else 2):
                        split_lo(nx, u)
                    for f in range(2):
                        done(nd + 3, 2 + f)
                        d.tensor_tensor(m[:, 6 + f, :], psum[:, 4 + f, :], m[:, 6 + f, :],
                                        ALU.add).then_inc(s["m_done"], 1)
                        if f == 0:
                            add_sq(3, 0)
                    if not last:
                        split_lo(nx, 2, single=True)

            mlp(0, N_MLP0, 1, False)
            boundary(1, V_FFN_POST, 2, V_MIX_PRE + 1)

            def q_evac(p):
                n = N_ATT + p
                done(n, 0)
                if not (isinstance(p, int) and p == 0):
                    dve.wait_ge(s["q_ready"], p)
                d.scalar_tensor_tensor(tmp[:, 0, :], psum[:, 0, :], -HD ** -0.5, rinv[:, :], ALU.mult,
                                       ALU.mult).then_inc(s["pr_evac"], 1)

            def q_lo(p):
                dve.wait_ge(s["q_hi"], p + 1)
                d.tensor_tensor(qlo[:, :], tmp[:, 0, :], qhi[:, :].bitcast(F32),
                                ALU.subtract).then_inc(s["q_ready"], 1)

            def k_evac(p):
                done(N_ATT + p, 1)
                if not (isinstance(p, int) and p == 0):
                    dve.wait_ge(s["k_ready"], 2 * p)
                d.tensor_tensor(tmp[:, 1, :], psum[:, 1, :], rinv[:, :], ALU.mult).then_inc(s["pr_evac"], 1)

            def k_lo(p):
                for hh in range(2):
                    rows = slice(HD * hh, HD * hh + HD)
                    dve.wait_ge(s["k_hi"], 2 * p + (hh + 1))
                    d.tensor_tensor(kzlo[rows, hh, :], tmp[rows, 1, :], kzhi[rows, hh, :].bitcast(F32),
                                    ALU.subtract).then_inc(s["k_ready"], 1)

            def v_evac(p):
                dve.wait_ge(unit[1], 2 * (N_ATT + p) + 4)
                if not (isinstance(p, int) and p == 0):
                    dve.wait_ge(s["vtr"], p)
                d.tensor_tensor(tmp[:, 2, :], psum[:, 2, :], rinv[:, :], ALU.mult).then_inc(s["pr_evac"], 1)

            dve.wait_ge(s["f_done"], 1)
            d.tensor_tensor(fwork[:, FZ, :], psum[:, 3, :], rinv[:, :], ALU.mult).then_inc(s["f_z"], 1)
            d.memset(tmp[:, 3, :], 1.0).then_inc(s["f_log"], 1)
            dve.wait_ge(s["f_z"], 1)
            dve.wait_ge(s["wf_loaded"], 80)
            d.tensor_scalar(fwork[:, FB, :], fwork[:, FZ, :], bf[:, 0:1], 0.0, ALU.add,
                            ALU.min).then_inc(s["f_b"], 1)
            q_evac(0)
            k_evac(0)
            v_evac(0)
            dve.wait_ge(s["f_b"], 1)
            dve.wait_ge(s["f_ln"], 1)
            d.tensor_tensor(fwork[:, FLOG, :], fwork[:, FB, :], fwork[:, FLN, :],
                            ALU.subtract).then_inc(s["f_log"], 1)
            dve.wait_ge(s["f_log"], 2)
            d.tensor_tensor_scan(fwork[:, FCUM, :], tmp[:, 3, :], fwork[:, FLOG, :], 0.0,
                                 ALU.mult, ALU.add).then_inc(s["f_cum"], 1)
            q_lo(0)
            k_lo(0)
            dve.wait_ge(s["f_hi"], 1)
            dve.wait_ge(s["f_base"], 6)
            d.tensor_tensor(fwork[:, FZ, :], fwork[:, FCUM, :], Fhi[:, :].bitcast(F32),
                            ALU.subtract).then_inc(s["f_lo"], 1)
            dve.wait_ge(s["f_lo"], 1)
            d.tensor_copy(rhsF[32:32 + HEADS, :], fwork[32:32 + HEADS, FZ, :]).then_inc(s["f_rows"], 1)
            d.tensor_scalar(lhsB[96:96 + HEADS, :], fwork[96:96 + HEADS, FZ, :], -1.0, None,
                            ALU.mult).then_inc(s["f_rows"], 1)
            for u in range(3):
                split_lo(N_ATT + 1, u, single=u == 2)

            def attention(p, project, units):
                def normalise(i):
                    hh, j = i // 4, i % 4
                    dve.wait_ge(s["ex_done"], 8 * p + (i + 1))
                    d.reciprocal(rden[:, i:i + 1], den[:, i:i + 1]).then_inc(s["rc_done"], 1)
                    dve.wait_ge(s["rc_done"], 8 * p + (i + 1))
                    pr = probs(hh, j)
                    d.tensor_scalar(pr, pr, rden[:, i:i + 1], None, ALU.mult).then_inc(s["p_ready"], 1)

                for what, i in SEQ:
                    hh, j = i // 4, i % 4
                    if what == "S":
                        dve.wait_ge(s["sc_done"], 8 * p + (i + 1))
                        dve.wait_ge(s["t_done"], 8 * p + (i + 1))
                        d.sem_inc(s["sc_seen"], 1)
                        d.tensor_tensor_reduce(out=probs(hh, j), in0=psum[:, SCORE + i % 2, 0:(j + 1) * P],
                                               in1=causal[:, S - (j + 1) * P:S], scale=1.0, scalar=3e38,
                                               op0=ALU.add, op1=ALU.min,
                                               accum_out=negmax[:, i:i + 1]).then_inc(s["sc_evac"], 1)
                        if i >= 1:
                            normalise(i - 1)
                        if i == 7:
                            normalise(7)
                    if what == "V":
                        dve.wait_ge(s["v_hi"], p + 1)
                        d.tensor_tensor(flat(vlo[:, :, :]), psum[:, 3, :], flat(vhi[:, :, :]).bitcast(F32),
                                        ALU.subtract).then_inc(s["v_ready"], 1)
                    if what == "EVAC" and project:
                        (q_evac, k_evac, v_evac)[i](p + 1)
                    if what == "PARTS" and project:
                        (q_lo, k_lo)[i](p + 1)
                    if what == "SPLIT" and project:
                        n = N_ATT + 2 + p
                        if units == 3:
                            split_lo(n, i, single=i == 2)
                        else:
                            for u in (i,) if i < 2 else (2, 3):
                                split_lo(n, u)
                    if what == "T":
                        dve.wait_ge(s["p_hi"], 8 * p + (i + 1))
                        src = psum[:, TRP[i % 2], 0:(j + 1) * P].rearrange("p (a b) -> p a b", b=P)
                        d.tensor_tensor(pTlo[:, 0:j + 1, j * P:(j + 1) * P], src,
                                        pThi[:, 0:j + 1, j * P:(j + 1) * P].bitcast(F32),
                                        ALU.subtract).then_inc(s["pt_ready"], 1)
                    if what == "O":
                        dve.wait_ge(s["o_hi"], 2 * p + (i + 1))
                        rows = slice(HD * i, HD * i + HD)
                        if isinstance(p, int):
                            dst, hi = olo[rows, p, :], ohi[rows, p, :]
                        else:
                            dst, hi = flat(olo[rows, ds(p, 1), :]), flat(ohi[rows, ds(p, 1), :])
                        d.tensor_tensor(dst, psum[rows, OUTP, :], hi.bitcast(F32),
                                        ALU.subtract).then_inc(s["o_ready"], 1)

            with dve.Fori(0, PAIRS - 2) as p:
                attention(p, True, 3)
            attention(PAIRS - 2, True, 4)
            attention(PAIRS - 1, False, 0)
            mixer_out(N_WO, 2)
            boundary(2, V_MIX_POST + 1, 3, V_FFN_PRE + 1)
            mlp(1, N_MLP1, 3, True)
            boundary(3, V_FFN_POST + 1, None, None)
            for k in range(KB):
                dve.wait_ge(s["out_tr"], k + 1)
                d.tensor_copy(outsb[:, :, k * P:(k + 1) * P],
                              psum[:, k % 2, :].rearrange("p (q c) -> p q c", c=P)
                              ).then_inc(s["out_copied"], 1)


_INS = ["x", "g_mix_pre", "g_mix_post", "g_ffn_pre", "g_ffn_post", "conv_pw1_w", "conv_pw1_b",
        "conv_dw_w", "conv_dw_b", "conv_ln_g", "conv_ln_b", "conv_pw2_w", "conv_pw2_b", "attn_w_in",
        "attn_b_f", "attn_w_o", "mlp_w_up", "mlp_w_down"]


def kernel(**inputs):
    import numpy as np
    import concourse.bacc as bacc
    from concourse import mybir as mb
    from concourse.bass_utils import run_bass_kernel_spmd as run

    nc = bacc.Bacc("TRN2", target_bir_lowering=False, num_devices=1)
    arrays, args = {}, []
    for name in _INS:
        a = np.ascontiguousarray(inputs[name])
        arrays[f"in_{name}"] = a
        args.append(nc.dram_tensor(f"in_{name}", a.shape, mb.dt.from_np(a.dtype),
                                   kind="ExternalInput").ap())
    args.append(nc.dram_tensor("out_x", (1, S, D), F32, kind="ExternalOutput").ap())
    build(nc, *args)
    r = run(nc, [arrays], core_ids=[0])
    return r.results[0]["out_x"]
```

```python
import concourse.bass as bass
from concourse import mybir

F32 = mybir.dt.float32
F32R = mybir.dt.float32r
ALU = mybir.AluOpType
ACT = mybir.ActivationFunctionType
ds = bass.ds

P = 128
D = 1024
S = 512
KB = D // P
TB = S // P
FF = 4 * D
HEADS = 16
HD = D // HEADS
PAIRS = HEADS // 2
W = 31
PADW = S + W + 1
PE_TAPS = 12
DVE_TAPS = W - PE_TAPS
MORE_TAPS = 6
WARM_SQ, WARM_ROOT, WARM_NORM, WARM_TAPS, WARM_SUB, WARM_START = 4, 5, 13, 4, 10, 20
MASK = 1e30
RMS_EPS = 1e-6
LN_EPS = 1e-5

N_PW1 = 0
N_PW2 = N_PW1 + 4
N_MLP0 = N_PW2 + 2
N_ATT = N_MLP0 + 16
N_WO = N_ATT + PAIRS
N_MLP1 = N_WO + 2
STEPS = N_MLP1 + 16

V_MIX_PRE, V_MIX_POST, V_FFN_PRE, V_FFN_POST = 0, 2, 4, 6
V_PW1B, V_DWB, V_LNG, V_LNB, V_PW2B, V_DW = 8, 10, 11, 12, 13, 14
V_ROWS = V_DW + W

ST_PRE = ("pre0", "pre1", "pre2", "pre3")
ST_POST = ("post0", "post1", "post2", "post3")
ST_VAR = "var"
NTH = {name: n + 1 for n, name in enumerate(
    ["pre0", "var", "post0", "pre1", "post1", "pre2", "post2", "pre3", "post3"])}
RINV_NTH = {name: n + 1 for n, name in enumerate(["pre0", "pre1", "pre2", "pre3"])}

SEQ = [("SPLIT", 2), ("P", 0), ("P", 1), ("S", 0), ("S", 1), ("V", 0), ("P", 2), ("S", 2), ("S", 3),
       ("P", 3), ("S", 4), ("S", 5), ("P", 4), ("S", 6), ("S", 7), ("P", 5), ("T", 0), ("P", 6),
       ("EVAC", 0), ("T", 1), ("PARTS", 0), ("T", 2), ("P", 7), ("T", 3), ("P", 8), ("SPLIT", 0),
       ("EVAC", 1), ("O", 0), ("T", 4), ("P", 9), ("PARTS", 1), ("T", 5), ("T", 6), ("P", 10),
       ("T", 7), ("P", 11), ("SPLIT", 1), ("AGAIN", 0), ("AGAIN", 1), ("O", 1), ("EVAC", 2)]
PARTS_OF_P = 12


def build(nc, x, g_mix_pre, g_mix_post, g_ffn_pre, g_ffn_post, conv_pw1_w, conv_pw1_b, conv_dw_w,
          conv_dw_b, conv_ln_g, conv_ln_b, conv_pw2_w, conv_pw2_b, attn_w_in, attn_b_f, attn_w_o,
          mlp_w_up, mlp_w_down, out):
    at = [0]
    base = (nc.sbuf_base + 63) // 64 * 64
    nc.alloc_sbuf_tensor("slab", [P, (nc.sbuf_usable_end - nc.sbuf_base - 256) // 4], F32)

    def put(name, shape, dt, where=None):
        n = 4
        for s in shape[1:]:
            n *= s
        pos = at[0] if where is None else where[0]
        t = nc.alloc_sbuf_tensor_at(name, shape, dt, offset=base + pos)
        if where is None:
            at[0] += (n + 31) // 32 * 32
        else:
            where[0] += (n + 31) // 32 * 32
        return t

    xT = put("xT", [P, KB, S], F32)
    at_h = [at[0]]
    hhi = put("hhi", [P, KB, S], F32R)
    at_out = [at[0]]
    hlo = put("hlo", [P, KB, S], F32R)
    m_wo = put("m_wo", [P, KB, S], F32, at_h)
    outsb = put("outsb", [P, TB, D], F32, at_out)
    wraw = put("wraw", [P, 2, KB, 2 * P], F32)
    whi = put("whi", [P, 4, KB, P], F32R)
    wlo = put("wlo", [P, 4, KB, P], F32R)
    at_m, at_m2 = [at[0]], [at[0]]
    m = put("m", [P, KB, S], F32)
    xin = put("xin", [P, TB, D], F32, at_m)
    ohi = put("ohi", [P, KB, S], F32R, at_m2)
    olo = put("olo", [P, KB, S], F32R)
    arena = at[0]
    ahi = put("ahi", [P, 16, S], F32R)
    alo = put("alo", [P, 16, S], F32R)
    ca = [arena]
    y = put("y", [P, KB, S], F32, ca)
    upad = put("upad", [P, 2, PADW], F32, ca)
    uhi = put("uhi", [P, 2, PADW], F32R, ca)
    ulo = put("ulo", [P, 2, PADW], F32R, ca)
    acc1 = put("acc1", [P, 2, S], F32, ca)
    dwhi = put("dwhi", [P, KB, MORE_TAPS + PE_TAPS], F32R, ca)
    dwlo = put("dwlo", [P, KB, MORE_TAPS + PE_TAPS], F32R, ca)
    cb = [ca[0]]
    diaghi = put("diaghi", [P, 2, PE_TAPS, P], F32R, ca)
    diaglo = put("diaglo", [P, 2, PE_TAPS, P], F32R, ca)
    vrows = put("vrows", [P, D], F32, cb)
    assert ca[0] <= at[0], (ca[0], at[0])
    aa = [arena]
    qa = put("qa", [P, 2, S], F32R, aa)
    ka = put("ka", [P, 2, S], F32R, aa)
    qb = put("qb", [P, 2, S], F32R, aa)
    k_b = put("kb", [P, 2, S], F32R, aa)
    own = (slice(0, HD), slice(HD, P))
    other = (own[1], own[0])
    vhi = put("vhi", [P, TB, P], F32R, aa)
    vlo = put("vlo", [P, TB, P], F32R, aa)
    prob = put("prob", [P, 2, 10 * P], F32, aa)
    gates_q = put("gates_q", [P, S], F32, aa)
    causal = put("causal", [P, S], F32, aa)
    ab, ac = [aa[0]], [aa[0]]
    pThi = put("pThi", [P, TB, S], F32R, aa)
    pTlo = put("pTlo", [P, TB, S], F32R, aa)
    wfhi = put("wfhi", [P, KB, P], F32R, ab)
    wflo = put("wflo", [P, KB, P], F32R, ab)
    Fhi = put("Fhi", [P, S], F32R, aa)
    fwork = put("fwork", [P, 8, S], F32, ac)
    KHI, KLO, QHI, QLO, K_ANY, Q_ANY, MINUS_QHI, MINUS_QLO = range(8)
    FZ, FB, FABS, FEXP, FLN, FLOG, FCUM, FONE = range(8)
    assert aa[0] <= at[0], (aa[0], at[0])
    tmp = put("tmp", [P, 4, S], F32)
    sumsq = put("sumsq", [P, S], F32)
    rinv = put("rinv", [P, S], F32)
    vec = put("vec", [P, KB, V_ROWS], F32)
    ident = put("ident", [P, P], F32)
    ones = put("ones", [P, P], F32)
    wfraw = put("wfraw", [P, KB, HEADS], F32)
    onehot = put("onehot", [P, HEADS], F32)
    group = put("group", [P, 8], F32)
    part = put("part", [P, 8], F32)
    bf = put("bf", [P, 1], F32)
    eps = put("eps", [P, 2], F32)
    negmax = put("negmax", [P, 8], F32)
    den = put("den", [P, 8], F32)
    rden = put("rden", [P, 8], F32)
    rms = put("rms", [P, TB], F32)
    unused = put("unused", [P, 8], F32)
    irms = put("irms", [P, TB], F32)
    assert base + at[0] <= nc.sbuf_usable_end - 256, (base + at[0], nc.sbuf_usable_end)

    psum = nc.alloc_psum_tensor("psum", [P, 8, 512], F32)
    STAT, SCORE, TRP, OUTP = 6, 4, (6, 3), 7

    sem_names = (
        "x_loaded0 x_loaded1 x_loaded2 x_loaded3 vec_loaded wf_loaded raw0 raw1 consts "
        "vt_done vec_ready xt_done xt_copied "
        "w_hi0 w_hi1 w_ready0 w_ready1 unit0 unit1 "
        "h_hi h_ready p_sq p_sum stat root irms_done spread bcast rinv_done "
        "m_done m_sq m_sum m_zero t1_done x_done "
        "glu_t glu_g glu_s glu_u u_hi u_ready dw_hi dw_lo diag conv_done tap_act tap acc y_done y_sum "
        "mean c_sub c_sq c_sum c_add c_pair c_nrm c_silu c_hi c_ready "
        "up_evac up_sq up_hi a_ready dn_evac "
        "wf_hi wf_ready f_done f_z f_b f_abs f_exp f_ln f_log f_cum f_hi f_lo f_one f_part f_rows f_base f_ready sel sel_part "
        "pr_evac q_hi q_ready k_hi k_ready vtr v_hi v_ready "
        "sc_done sc_seen sc_evac ex_done rc_done p_ready t_done p_hi pt_ready pv_done o_hi o_ready "
        "out_tr out_copied stored"
    ).split()
    s = {n: nc.alloc_semaphore(n) for n in sem_names}
    raw = (s["raw0"], s["raw1"])
    w_hi = (s["w_hi0"], s["w_hi1"])
    w_ready = (s["w_ready0"], s["w_ready1"])
    unit = (s["unit0"], s["unit1"])

    def flat(ap):
        return ap.rearrange("p a b -> p (a b)")

    def vcol(row, k):
        if isinstance(k, int):
            return vec[:, k, row:row + 1]
        return flat(vec[:, ds(k, 1), row:row + 1])

    def blk(t, k):
        if isinstance(k, int):
            return t[:, k, :]
        return flat(t[:, ds(k, 1), :])

    def probs(hh, j):
        o = P * (j * (j + 1) // 2)
        return prob[:, hh, o:o + P * (j + 1)]

    def mbuf(b):
        return m_wo if b == 2 else m

    with nc.Block() as block:

        @block.sync
        def _(sp):
            def load(n, r, parts):
                if not (isinstance(n, int) and n == 0):
                    sp.wait_ge(w_ready[r], 2 * n)
                for dst, src in parts:
                    sp.dma_start(dst, src).then_inc(raw[r], 16)

            def by_rows(w, r, col):
                wr = w.rearrange("(k p) f -> p k f", p=P)
                c = col if isinstance(col, int) else None
                sl = slice(c, c + 2 * P) if c is not None else ds(col, 2 * P)
                return [(wraw[:, r, 4 * k:4 * k + 4, :], wr[:, 4 * k:4 * k + 4, sl]) for k in range(2)]

            def by_cols(w, r, cols):
                wr = w.rearrange("(k p) f -> p k f", p=P)
                return [(wraw[:, r, :, P * c:P * c + P], wr[:, :, ds(cols[c], P)]) for c in range(2)]

            rows = [(V_MIX_PRE, 2, g_mix_pre), (V_MIX_POST, 2, g_mix_post), (V_FFN_PRE, 2, g_ffn_pre),
                    (V_FFN_POST, 2, g_ffn_post),
                    (V_PW1B, 2, conv_pw1_b.rearrange("a (b d) -> (a b) d", b=2)), (V_DWB, 1, conv_dw_b),
                    (V_LNG, 1, conv_ln_g), (V_LNB, 1, conv_ln_b), (V_PW2B, 1, conv_pw2_b),
                    (V_DW, W, conv_dw_w[0])]
            for row, n, src in rows:
                sp.dma_start(vrows[row:row + n, :], src).then_inc(s["vec_loaded"], 16)
            xr = x[0].rearrange("(q p) d -> p q d", p=P)
            for c in range(4):
                cols = slice(c * 2 * P, (c + 1) * 2 * P)
                sp.dma_start(xin[:, :, cols], xr[:, :, cols]).then_inc(s[f"x_loaded{c}"], 16)
            for n in range(1):
                for r in range(2):
                    load(n, r, by_cols(conv_pw1_w[0], r, [(2 * n + r) * P, D + (2 * n + r) * P]))
            for g in range(P // HEADS):
                sp.dma_start(bf[HEADS * g:HEADS * (g + 1), :],
                             attn_b_f.rearrange("a h -> h a")).then_inc(s["wf_loaded"], 16)
            sp.dma_start(wfraw[:, :, :],
                         attn_w_in[0].rearrange("(k p) f -> p k f", p=P)[:, :, 3 * D:3 * D + HEADS]
                         ).then_inc(s["wf_loaded"], 16)
            with sp.Fori(1, 4) as i:
                for r in range(2):
                    load(N_PW1 + i, r, by_cols(conv_pw1_w[0], r, [i * 256 + r * P, i * 256 + (D + r * P)]))
            for i in range(2):
                for r in range(2):
                    load(N_PW2 + i, r, by_rows(conv_pw2_w[0], r, (2 * i + r) * 2 * P))

            def mlp_loads(l, n0):
                for half in range(2):
                    with sp.Fori(0, 4) as i:
                        for r in range(2):
                            load(n0 + 8 * half + i, r,
                                 by_rows(mlp_w_up[l], r, i * 512 + (half * 2048 + r * 256)))
                    with sp.Fori(0, 4) as i:
                        for r in range(2):
                            rows_ = mlp_w_down[l, half * 2048 + r * D:half * 2048 + (r + 1) * D, :]
                            load(n0 + 8 * half + 4 + i, r, by_rows(rows_, r, i * 256))

            mlp_loads(0, N_MLP0)
            wv = attn_w_in[0].rearrange("(k p) f -> p k f", p=P)
            with sp.Fori(0, PAIRS) as i:
                load(N_ATT + i, 0, by_cols(attn_w_in[0], 0, [i * P, i * P + D]))
                load(N_ATT + i, 1, [(wraw[:, 1, 4 * k:4 * k + 4, 0:P],
                                     wv[:, 4 * k:4 * k + 4, ds(i * P + 2 * D, P)]) for k in range(2)])
            for i in range(2):
                for r in range(2):
                    load(N_WO + i, r, by_rows(attn_w_o[0], r, (2 * i + r) * 2 * P))
            mlp_loads(1, N_MLP1)
            od = out[0].rearrange("(q p) d -> p q d", p=P)
            stores = [(0, 2), (2, 4), (4, 6), (6, 7), (7, 8)]
            for k, end in stores:
                sp.wait_ge(s["out_copied"], end)
                sp.dma_start(od[:, :, k * P:end * P],
                             outsb[:, :, k * P:end * P]).then_inc(s["stored"], 16)
            sp.wait_ge(s["stored"], 16 * len(stores))

        @block.gpsimd
        def _(pool):
            g = nc.gpsimd
            g.memset(ident[:, :], 0.0).then_inc(s["consts"], 1)
            g.memset(ones[:, :], 1.0).then_inc(s["consts"], 1)
            g.memset(eps[:, 0:1], RMS_EPS).then_inc(s["consts"], 1)
            g.memset(eps[:, 1:2], LN_EPS).then_inc(s["consts"], 1)
            pool.wait_ge(s["consts"], 1)
            g.affine_select(out=ident[:, :], in_=ident[:, :], compare_op=ALU.not_equal, fill=1.0, base=0,
                            pattern=[[-1, P]], channel_multiplier=1).then_inc(s["consts"], 1)
            g.memset(upad[:, :, :], 0.0).then_inc(s["consts"], 1)
            g.memset(onehot[:, :], 0.0).then_inc(s["sel"], 1)
            for q in range(P // HEADS):
                pool.wait_ge(s["sel"], q + 1)
                g.affine_select(out=onehot[:, :], in_=onehot[:, :], compare_op=ALU.not_equal, fill=1.0,
                                base=-HEADS * q, pattern=[[-1, HEADS]],
                                channel_multiplier=1).then_inc(s["sel"], 1)
            g.memset(group[:, :], 1.0).then_inc(s["sel_part"], 1)
            for base, step, mult in ((0, -HEADS, 1), (HEADS - 1, HEADS, -1)):
                pool.wait_ge(s["sel_part"], 1 + (mult < 0))
                g.affine_select(out=group[:, :], in_=group[:, :], compare_op=ALU.is_ge, fill=0.0,
                                base=base, pattern=[[step, 8]],
                                channel_multiplier=mult).then_inc(s["sel_part"], 1)
            g.memset(part[:, :], 0.0).then_inc(s["sel_part"], 1)
            pool.wait_ge(s["sel_part"], 4)
            g.tensor_tensor(part[:, MINUS_QHI:MINUS_QLO + 1], part[:, MINUS_QHI:MINUS_QLO + 1],
                            group[:, QHI:QLO + 1], ALU.subtract).then_inc(s["sel_part"], 1)
            g.tensor_tensor(part[:, KHI:QLO + 1], group[:, 0:4], group[:, 4:8],
                            ALU.add).then_inc(s["sel_part"], 1)
            pool.wait_ge(s["sel_part"], 6)
            g.tensor_tensor(part[:, MINUS_QHI:MINUS_QLO + 1], part[:, MINUS_QHI:MINUS_QLO + 1],
                            group[:, 4 + QHI:4 + QLO + 1], ALU.subtract).then_inc(s["sel_part"], 1)
            g.tensor_tensor(part[:, K_ANY:K_ANY + 1], part[:, KHI:KHI + 1], part[:, KLO:KLO + 1],
                            ALU.add).then_inc(s["sel_part"], 1)
            g.tensor_tensor(part[:, Q_ANY:Q_ANY + 1], part[:, QHI:QHI + 1], part[:, QLO:QLO + 1],
                            ALU.add).then_inc(s["sel_part"], 1)
            def y_total(j):
                pool.wait_ge(s["y_done"], j + 1)
                pool.wait_ge(s["y_sum"], j + 1)
                yb = blk(y, j)
                g.tensor_tensor(sumsq[:, :], sumsq[:, :], yb, ALU.add).then_inc(s["y_sum"], 1)

            def add_squares(v):
                for k in range(KB):
                    pool.wait_ge(s["p_sq"], KB * v + k + 1)
                    sq = tmp[:, 2 + k % 2, :]
                    if k == 0:
                        g.tensor_copy(sumsq[:, :], sq).then_inc(s["p_sum"], 1)
                    else:
                        pool.wait_ge(s["p_sum"], KB * v + k)
                        g.tensor_tensor(sumsq[:, :], sumsq[:, :], sq, ALU.add).then_inc(s["p_sum"], 1)

            add_squares(0)
            pool.wait_ge(s["rinv_done"], 1)
            g.memset(sumsq[:, :], 0.0).then_inc(s["y_sum"], 1)
            with pool.Fori(0, KB - 1) as i:
                y_total(i)

            pool.wait_ge(s["c_sq"], 4)
            g.tensor_tensor(sumsq[:, :], m[:, 1, :], m[:, 3, :], ALU.add).then_inc(s["c_add"], 1)
            pool.wait_ge(s["c_add"], 1)
            pool.wait_ge(s["c_sq"], 6)
            g.tensor_tensor(sumsq[:, :], sumsq[:, :], m[:, 5, :], ALU.add).then_inc(s["c_add"], 1)
            add_squares(1)

            pool.wait_ge(unit[1], 2 * (N_MLP0 + 15) + 4)
            pool.wait_ge(s["wf_loaded"], 16 * (P // HEADS + 1))
            wsrc = wfraw[:, :, :]
            for q in range(P // HEADS):
                cols = slice(HEADS * q, HEADS * (q + 1))
                g.tensor_copy(wfhi[:, :, cols], wsrc).then_inc(s["wf_hi"], 1)
                pool.wait_ge(s["wf_hi"], q + 1)
                g.tensor_tensor(wflo[:, :, cols], wsrc, wfhi[:, :, cols].bitcast(F32),
                                ALU.subtract).then_inc(s["wf_ready"], 1)
            g.memset(fwork[:, FONE, :], 1.0).then_inc(s["f_one"], 1)
            g.memset(causal[:, :], 0.0).then_inc(s["f_base"], 1)
            pool.wait_ge(s["f_base"], 1)
            g.affine_select(out=causal[:, S - P:S], in_=causal[:, S - P:S], compare_op=ALU.is_ge,
                            fill=MASK, base=0, pattern=[[-1, P]],
                            channel_multiplier=1).then_inc(s["f_base"], 1)
            add_squares(2)
            pool.wait_ge(s["f_rows"], 3)
            def head_rows(h, hh):
                rows = other[hh]
                oh = onehot[rows, h:h + 1] if isinstance(h, int) else onehot[rows, ds(h, 1)]
                g.tensor_tensor(qb[rows, hh, :], gates_q[rows, :], oh.broadcast_to([HD, S]),
                                ALU.mult).then_inc(s["f_ready"], 1)
            pool.wait_ge(s["sel"], P // HEADS + 1)
            for hh in range(2):
                head_rows(hh, hh)
            with pool.Fori(1, PAIRS) as p:
                for hh in range(2):
                    pool.wait_ge(s["sc_done"], 8 * p + (4 * hh - 4))
                    head_rows(2 * p + hh, hh)
            add_squares(3)

        @block.tensor
        def _(pe):
            pe.sem_inc(unit[0], 2)
            pe.sem_inc(unit[1], 2)
            pe.sem_inc(s["t_done"], 8)
            pe.sem_inc(s["pv_done"], 1)

            def product(bank, u, kb, xhi, xlo, start, stop, cols=None):
                o = psum[:, bank, :]
                pe.matmul(o, whi[:, u, kb, :], xhi, start=start, stop=False)
                pe.matmul(o, whi[:, u, kb, :], xlo, start=False, stop=False)
                return pe.matmul(o, wlo[:, u, kb, :], xhi, start=False, stop=stop)

            def weights(n, u):
                pe.wait_ge(w_ready[u // 2], 2 * n + (1 + u % 2))

            def keep_warm(n, bank=OUTP):
                for _ in range(n):
                    pe.matmul(psum[:, bank, 0:P], ones[:, :], ones[:, :], start=True, stop=True)

            def first_step(n, ready, count, v=None, apart=2, stat_at=1, bcast_at=2, pairs=0):
                def block(kb, units):
                    pe.wait_ge(ready, count + kb + 1)
                    for u in units:
                        product(u, u, kb, hhi[:, kb, :], hlo[:, kb, :], kb == 0, False)
                for r in range(2):
                    weights(n, 2 * r)
                    weights(n, 2 * r + 1)
                    for kb in range(pairs):
                        block(kb, (2 * r, 2 * r + 1))
                for kb in range(pairs, KB - apart):
                    block(kb, range(4))
                pe.wait_ge(ready, count + KB)
                if v is not None and stat_at < 0:
                    pre_columns(v)
                for u in range(4):
                    for kb in range(KB - apart, KB):
                        mm = product(u, u, kb, hhi[:, kb, :], hlo[:, kb, :], False, kb == KB - 1)
                    mm.then_inc(unit[u // 2], 1)
                    if v is not None and u == stat_at:
                        pre_columns(v)
                    if v is not None and u == bcast_at:
                        broadcast(NTH[ST_PRE[v]])

            def whole_unit(n, u, xh=hhi, xl=hlo):
                weights(n, u)
                for kb in range(KB):
                    mm = product(u, u, kb, xh[:, kb, :], xl[:, kb, :], kb == 0, kb == KB - 1)
                mm.then_inc(unit[u // 2], 1)

            def columns(src, first, last, bank=STAT):
                for q in range(TB):
                    mm = pe.matmul(psum[:, bank, q:q + 1], src[:, q * P:(q + 1) * P], ones[:, 0:1],
                                   start=first and q == 0, stop=last, skip_group_check=True)
                return mm

            def broadcast(idx):
                pe.wait_ge(s["spread"], idx)
                pe.matmul(psum[:, STAT, :], ones[:, :], tmp[:, 0, :], start=True,
                          stop=True).then_inc(s["bcast"], 1)

            def pre_columns(v):
                pe.wait_ge(s["p_sum"], KB * (v + 1))
                columns(sumsq, True, True).then_inc(s["stat"], 1)

            def post_stat(b):
                keep_warm(WARM_SQ)
                pe.wait_ge(s["m_sum"], 7 * b + 9)
                columns(sumsq, True, False)
                pe.wait_ge(s["m_sq"], KB * (b + 1))
                columns(tmp[:, 3, :], False, True).then_inc(s["stat"], 1)
                keep_warm(WARM_ROOT)
                broadcast(NTH[ST_POST[b]])
                keep_warm(WARM_NORM)

            pe.wait_ge(s["consts"], 6)
            pe.wait_ge(s["vec_loaded"], 160)
            for k in range(KB):
                t = pe.transpose(psum[:, 7, k * V_ROWS:(k + 1) * V_ROWS], vrows[0:V_ROWS, k * P:(k + 1) * P],
                                 ident[0:V_ROWS, 0:V_ROWS])
            t.then_inc(s["vt_done"], 1)
            for k in range(KB):
                pe.wait_ge(s[f"x_loaded{k // 2}"], 16)
                if k == 3:
                    pe.wait_ge(s["vec_ready"], 1)
                if k >= 4:
                    pe.wait_ge(s["xt_copied"], k - 3)
                for q in range(TB):
                    t = pe.transpose(psum[:, 4 + k % 4, q * P:(q + 1) * P], xin[:, q, k * P:(k + 1) * P],
                                     ident[:, :])
                t.then_inc(s["xt_done"], 1)

            def conv(j, r, more=0):
                pe.wait_ge(s["u_ready"], j + 1)
                pe.wait_ge(s["diag"], j + 1)
                if not (isinstance(j, int) and j < 2):
                    pe.wait_ge(s["y_done"], j - 1)
                o = psum[:, 4 + r, :]
                taps = [(r, k, DVE_TAPS + k) for k in range(PE_TAPS)]
                taps += [(1 - r, k, DVE_TAPS - more + k) for k in range(more)]
                for k, (slot, at_, t) in enumerate(taps):
                    if k == PE_TAPS:
                        pe.wait_ge(s["diag"], KB + 1)
                    dh, dl = diaghi[:, slot, at_, :], diaglo[:, slot, at_, :]
                    xh, xl = uhi[:, r, t:t + S], ulo[:, r, t:t + S]
                    pe.matmul(o, dh, xh, start=k == 0, stop=False)
                    pe.matmul(o, dh, xl, start=False, stop=False)
                    mm = pe.matmul(o, dl, xh, start=False, stop=k == len(taps) - 1)
                mm.then_inc(s["conv_done"], 1)

            keep_warm(WARM_START, 0)
            first_step(N_PW1, s["h_ready"], 0, 0, apart=4, stat_at=-1, bcast_at=0, pairs=3)
            conv(0, 0)
            with pe.Fori(1, 4) as i:
                for r in range(2):
                    pe.wait_ge(s["glu_u"], 2 * i + (r - 1))
                    for u in (2 * r, 2 * r + 1):
                        whole_unit(N_PW1 + i, u)
                    conv(2 * i + (r - 1), 1 - r)
            conv(KB - 1, 1, MORE_TAPS)
            pe.wait_ge(s["y_sum"], KB)
            pe.matmul(psum[:, STAT, :], ones[:, :], sumsq[:, :], start=True, stop=False)
            keep_warm(WARM_TAPS)
            pe.wait_ge(s["y_done"], KB)
            pe.matmul(psum[:, STAT, :], ones[:, :], y[:, KB - 1, :], start=False,
                      stop=True).then_inc(s["mean"], 1)
            keep_warm(WARM_SUB, 0)
            for k in (0, 2, 4):
                pe.wait_ge(s["c_sq"], k + 1)
                columns(m[:, k, :], k == 0, False, 7)
                keep_warm(3, 0)
            pe.wait_ge(s["c_pair"], 1)
            columns(m[:, 7, :], False, False, 7)
            pe.wait_ge(s["c_add"], 2)
            columns(sumsq, False, True, 7).then_inc(s["c_sum"], 1)
            keep_warm(WARM_ROOT, 0)
            broadcast(NTH[ST_VAR])
            keep_warm(WARM_NORM, 0)

            first_step(N_PW2, s["c_ready"], 0)
            for u in range(4):
                pe.wait_ge(s["m_done"], u + 3)
                whole_unit(N_PW2 + 1, u)
            post_stat(0)

            def mlp(l, n0, v, b):
                for half in range(2):
                    q = 2 * l + half
                    if half == 0:
                        first_step(n0, s["h_ready"], KB * v, v)
                        i0 = 1
                    else:
                        i0 = 0
                    with pe.Fori(i0, 4) as i:
                        for u in range(4):
                            if q > 0 or i0 == 1:
                                pe.wait_ge(s["up_evac"], 4 * i + (16 * q - 4 + u + 1))
                            whole_unit(n0 + 8 * half + i, u)
                    if half == 1:
                        pe.wait_ge(s["dn_evac"], 8 * (l + 1) + 2)
                    with pe.Fori(0, 4) as i:
                        n = n0 + 8 * half + 4 + i
                        for u in range(4):
                            kg, f = u // 2, u % 2
                            weights(n, u)
                            pe.wait_ge(s["a_ready"], 16 * q + 8 * (kg + 1))
                            if kg == 0 and half == 0:
                                pe.wait_ge(s["dn_evac"], 2 * i + (8 * l + f + 1))
                            if kg == 0 and half == 1:
                                pe.wait_ge(s["m_done"], 2 * i + (8 * b + f + 1))
                            for kb in range(KB):
                                a = 8 * kg + kb
                                mm = product(4 + f, u, kb, ahi[:, a, :], alo[:, a, :],
                                             kg == 0 and kb == 0, kg == 1 and kb == KB - 1)
                            mm.then_inc(unit[u // 2], 1)
                post_stat(b)

            mlp(0, N_MLP0, 1, 1)

            for u in range(2):
                weights(N_ATT, u)
            pe.wait_ge(w_ready[1], 2 * N_ATT + 2)
            pe.wait_ge(s["wf_ready"], P // HEADS)

            def gate_product(kb):
                o = psum[:, 3, :]
                pe.matmul(o, wfhi[:, kb, :], hhi[:, kb, :], start=kb == 0, stop=False)
                pe.matmul(o, wfhi[:, kb, :], hlo[:, kb, :], start=False, stop=False)
                return pe.matmul(o, wflo[:, kb, :], hhi[:, kb, :], start=False, stop=kb == KB - 1)

            for kb in range(KB - 2):
                pe.wait_ge(s["h_ready"], 2 * KB + kb + 1)
                gate_product(kb)
                for u in range(3):
                    product(u, u, kb, hhi[:, kb, :], hlo[:, kb, :], kb == 0, False)
            pe.wait_ge(s["h_ready"], 3 * KB)
            for kb in (KB - 2, KB - 1):
                mm = gate_product(kb)
            mm.then_inc(s["f_done"], 1)
            pre_columns(2)
            for u in range(3):
                for kb in (KB - 2, KB - 1):
                    mm = product(u, u, kb, hhi[:, kb, :], hlo[:, kb, :], False, kb == KB - 1)
                mm.then_inc(unit[u // 2], 2 if u == 2 else 1)
                if u == 0:
                    broadcast(NTH[ST_PRE[2]])

            def attention(p, project, fill=None):
                for what, i in SEQ:
                    hh, j = i // 4, i % 4
                    if what == "S":
                        if i == 0:
                            for name, each in (("q_hi", 4), ("q_ready", 2), ("k_hi", 4), ("k_ready", 2)):
                                pe.wait_ge(s[name], each * p + each)
                        if j == 0:
                            pe.wait_ge(s["f_ready"], 2 * p + (hh + 1))
                        pe.wait_ge(s["sc_evac"], 8 * p + (i + 1))
                        n = P * (j + 1)
                        o = psum[:, SCORE + i % 2, 0:n]
                        qs = slice(j * P, (j + 1) * P)
                        pe.matmul(o, qa[:, hh, qs], ka[:, hh, 0:n], start=True, stop=False)
                        pe.matmul(o, qb[:, hh, qs], k_b[:, hh, 0:n], start=False,
                                  stop=True).then_inc(s["sc_done"], 1)
                    if what == "V":
                        pe.wait_ge(s["pr_evac"], 3 * p + 6)
                        pe.wait_ge(s["pt_ready"], 8 * p + 2)
                        for q in range(TB):
                            t = pe.transpose(psum[:, 3, q * P:(q + 1) * P], tmp[:, 2, q * P:(q + 1) * P],
                                             ident[:, :])
                        t.then_inc(s["vtr"], 1)
                    if what == "P" and fill:
                        for u, kb in fill[i]:
                            if kb == 0:
                                pe.wait_ge(s["pr_evac"], 3 * PAIRS + u + 1)
                                weights(N_WO, u)
                            if u == 0 and kb == KB - 2:
                                pe.wait_ge(s["o_ready"], 2 * (PAIRS - 2) + 3)
                            product(u, u, kb, ohi[:, kb, :], olo[:, kb, :], kb == 0, False)
                    if what == "P" and project:
                        u, part = i // 4, i % 4
                        n = N_ATT + 1 + p
                        if part == 0:
                            weights(n, u) if u < 2 else pe.wait_ge(w_ready[1], 2 * n + 2)
                            pe.wait_ge(s["pr_evac"], 3 * p + (3 + u + 1))
                        for kb in (2 * part, 2 * part + 1):
                            mm = product(u, u, kb, hhi[:, kb, :], hlo[:, kb, :], kb == 0, kb == KB - 1)
                        if part == 3:
                            mm.then_inc(unit[u // 2], 2 if u == 2 else 1)
                    if what == "T":
                        pe.wait_ge(s["p_ready"], 8 * p + (i + 1))
                        pe.wait_ge(s["pt_ready"], 8 * p + (i + 1))
                        if i == 1:
                            pe.wait_ge(s["v_ready"], p + 1)
                        pr = probs(hh, j)
                        for kb in range(j + 1):
                            t = pe.transpose(psum[:, TRP[i % 2], kb * P:(kb + 1) * P], pr[:, kb * P:(kb + 1) * P],
                                             ident[:, :])
                        t.then_inc(s["t_done"], 1)
                    if what == "O":
                        pe.wait_ge(s["v_ready"], p + 1)
                        pe.wait_ge(s["pt_ready"], 8 * p + (4 * i + 6))
                        pe.wait_ge(s["o_ready"], 2 * p + (i + 1))
                        for kb in range(TB):
                            o = psum[:, OUTP, kb * P:S]
                            ph, pl = pThi[:, kb, kb * P:S], pTlo[:, kb, kb * P:S]
                            pe.matmul(o, vhi[:, kb, :], ph, start=kb == 0, stop=False)
                            pe.matmul(o, vhi[:, kb, :], pl, start=False, stop=False)
                            mm = pe.matmul(o, vlo[:, kb, :], ph, start=False, stop=kb == TB - 1)
                        mm.then_inc(s["pv_done"], 1)

            with pe.Fori(0, PAIRS - 2) as p:
                attention(p, True)
            attention(PAIRS - 2, True)
            fill = [(u, kb) for u in range(3) for kb in range(KB - 1)]
            few = (2, 3, 4)
            cuts = [sum(1 if i in few else 2 for i in range(n)) for n in range(PARTS_OF_P + 1)]
            attention(PAIRS - 1, False, [fill[cuts[i]:cuts[i + 1]] for i in range(PARTS_OF_P)])

            weights(N_WO, 3)
            pe.wait_ge(s["pt_ready"], 8 * PAIRS + 2)
            for kb in range(3):
                product(3, 3, kb, ohi[:, kb, :], olo[:, kb, :], kb == 0, False)
            pe.wait_ge(s["o_ready"], 2 * PAIRS + 1)
            for u in range(3):
                product(u, u, KB - 1, ohi[:, KB - 1, :], olo[:, KB - 1, :], False,
                        True).then_inc(unit[u // 2], 1)
            for kb in range(3, KB):
                mm = product(3, 3, kb, ohi[:, kb, :], olo[:, kb, :], False, kb == KB - 1)
            mm.then_inc(unit[1], 1)
            for u in range(4):
                pe.wait_ge(s["m_done"], 16 + u + 3)
                whole_unit(N_WO + 1, u, ohi, olo)
            post_stat(2)
            mlp(1, N_MLP1, 3, 3)
            for k in range(KB):
                pe.wait_ge(s["x_done"], 3 * KB + k + 1)
                if k >= 2:
                    pe.wait_ge(s["out_copied"], k - 1)
                for q in range(TB):
                    t = pe.transpose(psum[:, k % 2, q * P:(q + 1) * P], xT[:, k, q * P:(q + 1) * P],
                                     ident[:, :])
                t.then_inc(s["out_tr"], 1)

        @block.scalar
        def _(act):
            a = nc.scalar

            def split_hi(n, u, single=False):
                r, c = u // 2, u % 2
                act.wait_ge(raw[r], 32 * n + 32)
                act.wait_ge(unit[r], 2 * n + (2 if single else 1 + c))
                a.activation(whi[:, u, :, :], wraw[:, r, :, c * P:(c + 1) * P],
                             ACT.Copy).then_inc(w_hi[r], 2 if single else 1)

            def done(n, u):
                act.wait_ge(unit[u // 2], 2 * n + (3 + u % 2))

            def square(src, k, sem_in, count, sem_free, free, sem_out):
                act.wait_ge(sem_in, count)
                if free is not None:
                    act.wait_ge(sem_free, free)
                a.activation(tmp[:, 2 + k % 2, :], src, ACT.Square).then_inc(sem_out, 1)

            def pre_norm(v, row, x_sem, x_count, also=None):
                for k in range(KB):
                    act.wait_ge(x_sem, x_count + k + 1)
                    a.activation(hhi[:, k, :], xT[:, k, :], ACT.Identity,
                                 scale=vcol(row, k)).then_inc(s["h_hi"], 1)
                    square(xT[:, k, :], k, x_sem, x_count + k + 1, s["p_sum"],
                           KB * v + k - 1 if k > 1 else None, s["p_sq"])
                    if also:
                        also(k)

            def root(idx, e=0, bank=STAT):
                if idx == ST_VAR:
                    act.wait_ge(s["c_sum"], 1)
                else:
                    act.wait_ge(s["stat"], NTH[idx] - (NTH[idx] > NTH[ST_VAR]))
                a.activation(rms[:, :], psum[:, bank, 0:TB], ACT.Sqrt, scale=1.0 / D,
                             bias=eps[:, e:e + 1]).then_inc(s["root"], 1)

            def fetch_table(n, func):
                a.activation(unused[:, n:n + 1], eps[:, 0:1], func)

            def keep_row(idx):
                act.wait_ge(s["bcast"], NTH[idx])
                a.activation(rinv[:, :], psum[:, STAT, :], ACT.Copy).then_inc(s["rinv_done"], 1)

            def diagonals(j, r, more=False):
                for k in range(MORE_TAPS if more else PE_TAPS):
                    for dst, src in ((diaghi, dwhi), (diaglo, dwlo)):
                        c = k + (0 if more else MORE_TAPS)
                        col = src[:, j, c:c + 1] if isinstance(j, int) else flat(src[:, ds(j, 1), c:c + 1])
                        i_ = a.activation(dst[:, r, k, :], ident[:, :], ACT.Identity,
                                          scale=col.bitcast(F32))
                i_.then_inc(s["diag"], 1)

            act.wait_ge(s["consts"], 4)
            fetch_table(6, ACT.Sqrt)
            act.wait_ge(s["vec_ready"], 1)
            a.activation(dwhi[:, :, :], vec[:, :, V_DW + DVE_TAPS - MORE_TAPS:V_DW + W],
                         ACT.Copy).then_inc(s["dw_hi"], 1)
            pre_norm(0, V_MIX_PRE, s["xt_copied"], 0, 
                     lambda k: [split_hi(0, u) for u in {2: (0, 1), 3: (2, 3)}.get(k, ())])
            act.wait_ge(s["dw_lo"], 1)
            diagonals(0, 0)
            root(ST_PRE[0])
            fetch_table(0, ACT.Sigmoid)
            keep_row(ST_PRE[0])

            def conv_step(n, last=False):
                for r in range(2):
                    j = 2 * n + r
                    act.wait_ge(s["glu_g"], j + 1)
                    a.activation(tmp[:, 1, :], tmp[:, 0, :], ACT.Sigmoid, bias=vcol(V_PW1B + 1, j)
                                 ).then_inc(s["glu_s"], 1)
                    act.wait_ge(s["glu_u"], j + 1)
                    if not (isinstance(j, int) and j < 2):
                        act.wait_ge(s["conv_done"], j - 1)
                    a.activation(uhi[:, r, :], upad[:, r, :], ACT.Copy).then_inc(s["u_hi"], 1)
                    if not (isinstance(j, int) and j < 2):
                        act.wait_ge(s["y_done"], j - 1)
                    a.activation(blk(y, j), upad[:, r, 0:S], ACT.Identity, scale=vcol(V_DW, j),
                                 bias=vcol(V_DWB, j)).then_inc(s["tap_act"], 1)
                    a.activation(acc1[:, r, :], upad[:, r, 1:1 + S], ACT.Identity,
                                 scale=vcol(V_DW + 1, j)).then_inc(s["tap_act"], 1)
                    for c in range(2):
                        split_hi(n + 1, 2 * r + c)
                    if not (last and r == 1):
                        if not (isinstance(j, int) and j < 1):
                            act.wait_ge(s["conv_done"], j)
                        diagonals(j + 1, 1 - r)
            conv_step(0)
            with act.Fori(1, 3) as i:
                conv_step(i)
            conv_step(3, last=True)
            act.wait_ge(s["conv_done"], KB - 1)
            diagonals(KB - 1, 0, True)
            fetch_table(1, ACT.Sqrt)
            for k in range(KB):
                act.wait_ge(s["c_sub"], k + 1)
                a.activation(m[:, k, :], y[:, k, :], ACT.Square).then_inc(s["c_sq"], 1)
            root(ST_VAR, 1, 7)
            for k in range(KB):
                act.wait_ge(s["c_nrm"], k + 1)
                if k >= 2:
                    act.wait_ge(s["c_ready"], k - 1)
                a.activation(tmp[:, k % 2, :], y[:, k, :], ACT.Silu, scale=vcol(V_LNG, k),
                             bias=vcol(V_LNB, k)).then_inc(s["c_silu"], 1)
                act.wait_ge(s["c_silu"], k + 1)
                a.activation(hhi[:, k, :], tmp[:, k % 2, :], ACT.Copy).then_inc(s["c_hi"], 1)

            def mixer_out(n0, b, dst, bias_row):
                for i in range(2):
                    for u in range(4):
                        k = 4 * i + u
                        done(n0 + i, u)
                        if bias_row is None:
                            e = a.activation(dst[:, k, :], psum[:, u, :], ACT.Copy)
                        else:
                            e = a.activation(dst[:, k, :], psum[:, u, :], ACT.Identity,
                                             bias=vcol(bias_row, k))
                        e.then_inc(s["m_done"], 1)
                        square(dst[:, k, :], k, s["m_done"], KB * b + k + 3, s["m_sum"],
                               7 * b + k + 1, s["m_sq"])
                        if k < KB - 1:
                            split_hi(n0 + i + 1, u)
                root(ST_POST[b])
                split_hi(n0 + 2, 3)

            fetch_table(2, ACT.Sqrt)
            mixer_out(N_PW2, 0, m, V_PW2B)

            def mlp(l, n0, b, last):
                v = 1 if l == 0 else 3
                pre_norm(v, V_FFN_PRE + l, s["x_done"], KB * (b - 1))
                split_hi(n0 + 1, 0)
                split_hi(n0 + 1, 1)
                root(ST_PRE[v])
                split_hi(n0 + 1, 2)
                keep_row(ST_PRE[v])
                for half in range(2):
                    q = 2 * l + half
                    def up(i, first=False):
                        for u in range(4):
                            act.wait_ge(s["up_sq"], 4 * i + (16 * q + u + 1))
                            a.activation(blk(ahi, 4 * i + u), tmp[:, 2 + u % 2, :],
                                         ACT.Copy).then_inc(s["up_hi"], 1)
                            if not first:
                                split_hi(n0 + 8 * half + i + 1, u)
                            elif u == 0:
                                split_hi(n0 + 1, 3)
                    if half == 0:
                        up(0, True)
                    with act.Fori(1 - half, 4) as i:
                        up(i)
                    nd = n0 + 8 * half + 4
                    def down(i):
                        for u in range(4):
                            if u >= 2:
                                f = u - 2
                                if half == 0:
                                    done(nd + i, u)
                                    a.activation(blk(m, 2 * i + f), psum[:, 4 + f, :],
                                                 ACT.Copy).then_inc(s["dn_evac"], 1)
                                else:
                                    square(blk(m, 2 * i + f), f, s["m_done"], 2 * i + (KB * b + f + 3),
                                           s["m_sum"], 2 * i + (7 * b + f + 1), s["m_sq"])
                            split_hi(nd + i + 1, u)
                    if half == 0:
                        with act.Fori(0, 4) as i:
                            down(i)
                        continue
                    with act.Fori(0, 3) as i:
                        down(i)
                    nx = nd + 4
                    for u in range(0 if last else 2):
                        split_hi(nx, u)
                    for f in range(2):
                        square(m[:, 6 + f, :], f, s["m_done"], 6 + KB * b + f + 3,
                               s["m_sum"], 6 + 7 * b + f + 1, s["m_sq"])
                    root(ST_POST[b])
                    if not last:
                        split_hi(nx, 2, single=True)

            a.sem_inc(s["dn_evac"], 2)
            mlp(0, N_MLP0, 1, False)
            pre_norm(2, V_MIX_PRE + 1, s["x_done"], KB)
            root(ST_PRE[2])
            fetch_table(3, ACT.Exp)
            keep_row(ST_PRE[2])

            def q_hi(p):
                act.wait_ge(s["pr_evac"], 3 * p + 4)
                if not (isinstance(p, int) and p == 0):
                    act.wait_ge(s["sc_done"], 8 * p)
                for hh in range(2):
                    a.activation(qa[own[hh], hh, :], tmp[own[hh], 0, :], ACT.Copy).then_inc(s["q_hi"], 1)

            def q_again(p):
                for hh in range(2):
                    a.activation(qb[own[hh], hh, :], tmp[own[hh], 0, :], ACT.Copy).then_inc(s["q_hi"], 1)

            def k_hi(p):
                act.wait_ge(s["pr_evac"], 3 * p + 5)
                for hh in range(2):
                    a.activation(ka[own[hh], hh, :], tmp[own[hh], 1, :], ACT.Copy).then_inc(s["k_hi"], 1)

            def k_again(p):
                for hh in range(2):
                    a.activation(ka[other[hh], hh, :], tmp[own[hh], 1, :], ACT.Copy).then_inc(s["k_hi"], 1)

            split_hi(N_ATT + 1, 0)
            act.wait_ge(s["f_z"], 1)
            act.wait_ge(s["wf_loaded"], 16 * (P // HEADS + 1))
            a.activation(fwork[:, FABS, :], fwork[:, FZ, :], ACT.Abs, bias=bf[:, 0:1]).then_inc(s["f_abs"], 1)
            act.wait_ge(s["f_abs"], 1)
            a.activation(fwork[:, FEXP, :], fwork[:, FABS, :], ACT.Exp, scale=-1.0).then_inc(s["f_exp"], 1)
            act.wait_ge(s["f_exp"], 1)
            a.activation(fwork[:, FLN, :], fwork[:, FEXP, :], ACT.Ln, bias=1.0).then_inc(s["f_ln"], 1)
            q_hi(0)
            k_hi(0)
            act.wait_ge(s["f_cum"], 1)
            a.activation(Fhi[:, :], fwork[:, FCUM, :], ACT.Copy).then_inc(s["f_hi"], 1)
            act.wait_ge(s["f_hi"], 1)
            act.wait_ge(s["sel_part"], 9)
            for dst, mult, add in ((FEXP, MINUS_QHI, K_ANY), (FABS, KHI, Q_ANY)):
                a.activation(fwork[:, dst, :], Fhi[:, :].bitcast(F32), ACT.Identity,
                             scale=part[:, mult:mult + 1], bias=part[:, add:add + 1]
                             ).then_inc(s["f_part"], 1)
            q_again(0)
            k_again(0)
            fetch_table(4, ACT.Exp)
            split_hi(N_ATT + 1, 1)

            def attention(p, project):
                for what, i in SEQ:
                    hh, j = i // 4, i % 4
                    if what == "S":
                        act.wait_ge(s["sc_evac"], 8 * p + (i + 3))
                        pr = probs(hh, j)
                        a.activation(pr, pr, ACT.Exp, scale=-1.0, bias=negmax[:, i:i + 1],
                                     accum_out=den[:, i:i + 1]).then_inc(s["ex_done"], 1)
                    if what == "V":
                        act.wait_ge(s["vtr"], p + 1)
                        act.wait_ge(s["pv_done"], 2 * p + 1)
                        a.activation(flat(vhi[:, :, :]), psum[:, 3, :], ACT.Copy).then_inc(s["v_hi"], 1)
                    if what == "PARTS" and project:
                        (q_hi, k_hi)[i](p + 1)
                    if what == "AGAIN" and project:
                        (q_again, k_again)[i](p + 1)
                    if what == "SPLIT" and project:
                        if i < 2:
                            split_hi(N_ATT + 2 + p, i)
                        else:
                            split_hi(N_ATT + 1 + p, 2, single=True)
                    if what == "SPLIT" and not project and i == 2:
                        split_hi(N_WO, 2)
                        split_hi(N_WO, 3)
                    if what == "T":
                        act.wait_ge(s["t_done"], 8 * p + (i + 9))
                        if j == 0:
                            act.wait_ge(s["pv_done"], 2 * p + (hh + 1))
                        src = psum[:, TRP[i % 2], 0:(j + 1) * P].rearrange("p (a b) -> p a b", b=P)
                        a.activation(pThi[:, 0:j + 1, j * P:(j + 1) * P], src,
                                     ACT.Copy).then_inc(s["p_hi"], 1)
                    if what == "O":
                        act.wait_ge(s["pv_done"], 2 * p + (i + 2))
                        rows = slice(HD * i, HD * i + HD)
                        dst = ohi[rows, p, :] if isinstance(p, int) else flat(ohi[rows, ds(p, 1), :])
                        a.activation(dst, psum[rows, OUTP, :], ACT.Copy).then_inc(s["o_hi"], 1)

            with act.Fori(0, PAIRS - 2) as p:
                attention(p, True)
            attention(PAIRS - 2, True)
            attention(PAIRS - 1, False)
            fetch_table(5, ACT.Sqrt)
            mixer_out(N_WO, 2, m_wo, None)
            mlp(1, N_MLP1, 3, True)
            for k in range(KB):
                act.wait_ge(s["out_tr"], k + 1)
                a.activation(outsb[:, :, k * P:(k + 1) * P],
                             psum[:, k % 2, :].rearrange("p (q c) -> p q c", c=P),
                             ACT.Copy).then_inc(s["out_copied"], 1)

        @block.vector
        def _(dve):
            d = nc.vector

            def split_lo(n, u, single=False):
                r, c = u // 2, u % 2
                dve.wait_ge(w_hi[r], 2 * n + (2 if single else 1 + c))
                d.tensor_tensor(wlo[:, u, :, :], wraw[:, r, :, c * P:(c + 1) * P],
                                whi[:, u, :, :].bitcast(F32), ALU.subtract
                                ).then_inc(w_ready[r], 2 if single else 1)

            def done(n, u):
                dve.wait_ge(unit[u // 2], 2 * n + (3 + u % 2))

            def h_lo(v, row, k):
                dve.wait_ge(s["h_hi"], KB * v + k + 1)
                d.scalar_tensor_tensor(hlo[:, k, :], xT[:, k, :], vcol(row, k), hhi[:, k, :].bitcast(F32),
                                       ALU.mult, ALU.subtract).then_inc(s["h_ready"], 1)

            def add_square(k, sem_in, count, sem_out, prev):
                dve.wait_ge(sem_in, count)
                if k == 0:
                    d.tensor_copy(sumsq[:, :], tmp[:, 2 + k % 2, :]).then_inc(sem_out, 1)
                else:
                    dve.wait_ge(sem_out, prev)
                    d.tensor_tensor(sumsq[:, :], sumsq[:, :], tmp[:, 2 + k % 2, :],
                                    ALU.add).then_inc(sem_out, 1)

            def inverse(idx):
                dve.wait_ge(s["root"], NTH[idx])
                d.reciprocal(irms[:, :], rms[:, :]).then_inc(s["irms_done"], 1)
                dve.wait_ge(s["irms_done"], NTH[idx])
                idb = ident[:, :].rearrange("p (a c) -> p a c", a=1).broadcast_to([P, TB, P])
                col = irms[:, :].rearrange("p (a c) -> p a c", c=1).broadcast_to([P, TB, P])
                d.tensor_tensor(tmp[:, 0, :].rearrange("p (a c) -> p a c", c=P), idb, col,
                                ALU.mult).then_inc(s["spread"], 1)

            d.sem_inc(s["m_done"], 2)
            d.sem_inc(s["m_sum"], 2)
            d.sem_inc(s["sc_evac"], 2)
            d.sem_inc(s["pt_ready"], 2)
            d.sem_inc(s["o_ready"], 1)
            d.sem_inc(s["pr_evac"], 3)
            dve.wait_ge(s["vt_done"], 1)
            d.tensor_copy(flat(vec[:, :, :]), psum[:, 7, 0:KB * V_ROWS]).then_inc(s["vec_ready"], 1)
            for k in range(KB + 3):
                if k < KB:
                    dve.wait_ge(s["xt_done"], k + 1)
                    d.tensor_copy(xT[:, k, :], psum[:, 4 + k % 4, :]).then_inc(s["xt_copied"], 1)
                if k >= 3:
                    h_lo(0, V_MIX_PRE, k - 3)
                for u in {5: (0, 1), 6: (2, 3)}.get(k, ()):
                    split_lo(0, u)
            dve.wait_ge(s["dw_hi"], 1)
            d.tensor_tensor(dwlo[:, :, :], vec[:, :, V_DW + DVE_TAPS - MORE_TAPS:V_DW + W], dwhi[:, :, :].bitcast(F32),
                            ALU.subtract).then_inc(s["dw_lo"], 1)
            inverse(ST_PRE[0])

            def tap(j, r, t):
                dst = blk(y, j) if t % 2 == 0 else acc1[:, r, :]
                if t < 4:
                    dve.wait_ge(s["tap_act"], 2 * j + (t - 1))
                else:
                    dve.wait_ge(s["tap"], (DVE_TAPS - 2) * j + (t - 3))
                d.scalar_tensor_tensor(dst, upad[:, r, t:t + S], vcol(V_DW + t, j), dst, ALU.mult,
                                       ALU.add).then_inc(s["tap"], 1)

            def gates(n, r):
                j = 2 * n + r
                if isinstance(j, int) and j == 0:
                    dve.wait_ge(s["rinv_done"], RINV_NTH[ST_PRE[0]])
                done(N_PW1 + n, 2 * r + 1)
                if not (isinstance(j, int) and j == 0):
                    dve.wait_ge(s["glu_u"], j)
                d.tensor_tensor(tmp[:, 0, :], psum[:, 2 * r + 1, :], rinv[:, :],
                                ALU.mult).then_inc(s["glu_g"], 1)
                d.tensor_tensor(tmp[:, 2, :], psum[:, 2 * r, :], rinv[:, :],
                                ALU.mult).then_inc(s["glu_t"], 1)

            def gated(j, r):
                dve.wait_ge(s["glu_t"], j + 1)
                dve.wait_ge(s["glu_s"], j + 1)
                if isinstance(j, int) and j < 2:
                    dve.wait_ge(s["consts"], 6)
                else:
                    dve.wait_ge(s["u_ready"], j - 1)
                d.scalar_tensor_tensor(upad[:, r, W - 1:W - 1 + S], tmp[:, 2, :], vcol(V_PW1B, j),
                                       tmp[:, 1, :], ALU.add, ALU.mult).then_inc(s["glu_u"], 1)

            def u_lo(j, r):
                dve.wait_ge(s["u_hi"], j + 1)
                d.tensor_tensor(ulo[:, r, :], upad[:, r, :], uhi[:, r, :].bitcast(F32),
                                ALU.subtract).then_inc(s["u_ready"], 1)

            def join(j, r, less=0):
                dve.wait_ge(s["tap"], (DVE_TAPS - 2) * (j + 1) - less)
                d.tensor_tensor(acc1[:, r, :], acc1[:, r, :], blk(y, j), ALU.add).then_inc(s["acc"], 1)

            def finish(j, r):
                dve.wait_ge(s["acc"], j + 1)
                dve.wait_ge(s["conv_done"], j + 1)
                d.tensor_tensor(blk(y, j), psum[:, 4 + r, :], acc1[:, r, :], ALU.add
                                ).then_inc(s["y_done"], 1)

            def conv_block(n, r, between=None):
                j = 2 * n + r
                gates(n, r)
                if not (isinstance(j, int) and j == 0):
                    join(j - 1, 1 - r)
                gated(j, r)
                if not (isinstance(j, int) and j == 0):
                    finish(j - 1, 1 - r)
                u_lo(j, r)
                for t in range(2, DVE_TAPS):
                    tap(j, r, t)
                    if t == DVE_TAPS // 2:
                        split_lo(n + 1, 2 * r)
                    if between:
                        between(t)
                if not between:
                    split_lo(n + 1, 2 * r + 1)

            for r in range(2):
                conv_block(0, r)
            with dve.Fori(1, 3) as i:
                for r in range(2):
                    conv_block(i, r)

            def last_gates(t):
                if t == 10:
                    gates(3, 1)
                if t == 11:
                    gated(KB - 1, 1)
                if t == 12:
                    u_lo(KB - 1, 1)
            conv_block(3, 0, last_gates)
            join(KB - 2, 0)
            finish(KB - 2, 0)
            for t in range(2, DVE_TAPS - MORE_TAPS):
                tap(KB - 1, 1, t)
            join(KB - 1, 1, MORE_TAPS)
            finish(KB - 1, 1)
            dve.wait_ge(s["mean"], 1)
            for k in range(KB):
                d.scalar_tensor_tensor(y[:, k, :], psum[:, STAT, :], -1.0 / D, y[:, k, :], ALU.mult,
                                       ALU.add).then_inc(s["c_sub"], 1)
            dve.wait_ge(s["c_sq"], KB)
            d.tensor_tensor(m[:, 7, :], m[:, 6, :], m[:, 7, :], ALU.add).then_inc(s["c_pair"], 1)
            for u in (1, 2):
                split_lo(N_PW2, u)
            inverse(ST_VAR)
            split_lo(N_PW2, 3)
            dve.wait_ge(s["bcast"], NTH[ST_VAR])
            for k in range(KB + 1):
                if k < KB:
                    d.tensor_tensor(y[:, k, :], y[:, k, :], psum[:, STAT, :], ALU.mult
                                    ).then_inc(s["c_nrm"], 1)
                if k >= 1:
                    dve.wait_ge(s["c_hi"], k)
                    d.tensor_tensor(hlo[:, k - 1, :], tmp[:, (k - 1) % 2, :], hhi[:, k - 1, :].bitcast(F32),
                                    ALU.subtract).then_inc(s["c_ready"], 1)

            def mixer_out(n0, b):
                for i in range(2):
                    for u in range(4):
                        k = 4 * i + u
                        if k < KB - 1:
                            add_square(k, s["m_sq"], KB * b + k + 1, s["m_sum"], 7 * b + k + 2)
                            split_lo(n0 + i + 1, u)

            def boundary(b, row_post, v, row_pre, n_next=None):
                inverse(ST_POST[b])
                if b in (0, 2):
                    split_lo(N_MLP0 if b == 0 else N_MLP1, 3)
                dve.wait_ge(s["bcast"], NTH[ST_POST[b]])
                src = mbuf(b)
                def scaled(k):
                    c = KB * b + k
                    if c >= 2:
                        dve.wait_ge(s["x_done"], c - 1)
                    d.scalar_tensor_tensor(tmp[:, k % 2, :], src[:, k, :], vcol(row_post, k),
                                           psum[:, STAT, :], ALU.mult, ALU.mult).then_inc(s["t1_done"], 1)
                ahead = 1 if v is None else 0
                if ahead:
                    scaled(0)
                for k in range(KB + 1):
                    c = KB * b + k
                    if k + ahead < KB:
                        scaled(k + ahead)
                    if k < KB:
                        dve.wait_ge(s["t1_done"], c + 1)
                        d.tensor_tensor(xT[:, k, :], xT[:, k, :], tmp[:, k % 2, :],
                                        ALU.add).then_inc(s["x_done"], 1)
                    if k >= 1 and v is not None:
                        h_lo(v, row_pre, k - 1)
                if v is not None:
                    if v != 2:
                        split_lo(n_next, 0)
                    inverse(ST_PRE[v])
                    if v != 2:
                        split_lo(n_next, 1)
                    dve.wait_ge(s["rinv_done"], RINV_NTH[ST_PRE[v]])

            mixer_out(N_PW2, 0)
            boundary(0, V_MIX_POST, 1, V_FFN_PRE, N_MLP0 + 1)

            def mlp(l, n0, b, last):
                for half in range(2):
                    q = 2 * l + half
                    def a_lo(i, u):
                        dve.wait_ge(s["up_hi"], 4 * i + (16 * q + u + 1))
                        d.tensor_tensor(blk(alo, 4 * i + u), tmp[:, 2 + u % 2, :],
                                        blk(ahi, 4 * i + u).bitcast(F32),
                                        ALU.subtract).then_inc(s["a_ready"], 1)
                    def up(i, peeled):
                        n = n0 + 8 * half + i
                        for u in range(4):
                            c = 4 * i + (16 * q + u)
                            done(n, u)
                            if not (q == 0 and peeled and u == 0):
                                dve.wait_ge(s["up_sq"], c)
                            d.tensor_tensor(tmp[:, 0, :], psum[:, u, :], rinv[:, :],
                                            ALU.mult).then_inc(s["up_evac"], 1)
                            dve.wait_ge(s["up_evac"], c + 1)
                            if not (q == 0 and peeled and u < 2):
                                dve.wait_ge(s["a_ready"], c - 1)
                            d.scalar_tensor_tensor(tmp[:, 2 + u % 2, :], tmp[:, 0, :], 0.0, tmp[:, 0, :],
                                                   ALU.max, ALU.mult).then_inc(s["up_sq"], 1)
                            if u >= 1:
                                a_lo(i, u - 1)
                            if not (half == 0 and peeled):
                                split_lo(n + 1, u)
                            elif u < 2:
                                split_lo(n + 1, u + 2)
                        a_lo(i, 3)
                    up(0, True)
                    with dve.Fori(1, 4) as i:
                        up(i, False)
                    nd = n0 + 8 * half + 4
                    if half == 0:
                        with dve.Fori(0, 4) as i:
                            for u in range(4):
                                split_lo(nd + i + 1, u)
                        continue
                    d.memset(sumsq[:, :], 0.0).then_inc(s["m_zero"], 1)
                    dve.wait_ge(s["m_zero"], l + 1)
                    def add_sq(i, f):
                        dve.wait_ge(s["m_sq"], 2 * i + (KB * b + f + 1))
                        dve.wait_ge(s["m_sum"], 2 * i + (7 * b + f + 2))
                        d.tensor_tensor(sumsq[:, :], sumsq[:, :], tmp[:, 2 + f, :],
                                        ALU.add).then_inc(s["m_sum"], 1)
                    def down(i):
                        for u in range(4):
                            if u >= 2:
                                f = u - 2
                                done(nd + i, u)
                                mb = blk(m, 2 * i + f)
                                d.tensor_tensor(mb, psum[:, 4 + f, :], mb, ALU.add).then_inc(s["m_done"], 1)
                            if u == 3:
                                add_sq(i, 0)
                            split_lo(nd + i + 1, u)
                        add_sq(i, 1)
                    dve.wait_ge(s["dn_evac"], 8 * (l + 1) + 2)
                    with dve.Fori(0, 3) as i:
                        down(i)
                    nx = nd + 4
                    for u in range(0 if last else 2):
                        split_lo(nx, u)
                    for f in range(2):
                        done(nd + 3, 2 + f)
                        d.tensor_tensor(m[:, 6 + f, :], psum[:, 4 + f, :], m[:, 6 + f, :],
                                        ALU.add).then_inc(s["m_done"], 1)
                        if f == 0:
                            add_sq(3, 0)
                    if not last:
                        split_lo(nx, 2, single=True)

            mlp(0, N_MLP0, 1, False)
            boundary(1, V_FFN_POST, 2, V_MIX_PRE + 1)

            def q_evac(p):
                n = N_ATT + p
                done(n, 0)
                if not (isinstance(p, int) and p == 0):
                    dve.wait_ge(s["q_ready"], 2 * p)
                    dve.wait_ge(s["q_hi"], 4 * p)
                d.scalar_tensor_tensor(tmp[:, 0, :], psum[:, 0, :], -HD ** -0.5, rinv[:, :], ALU.mult,
                                       ALU.mult).then_inc(s["pr_evac"], 1)

            def q_lo(p):
                for hh in range(2):
                    dve.wait_ge(s["q_hi"], 4 * p + (hh + 1))
                    d.tensor_tensor(qa[other[hh], hh, :], tmp[own[hh], 0, :], qa[own[hh], hh, :].bitcast(F32),
                                    ALU.subtract).then_inc(s["q_ready"], 1)

            def k_evac(p):
                done(N_ATT + p, 1)
                if not (isinstance(p, int) and p == 0):
                    dve.wait_ge(s["k_ready"], 2 * p)
                    dve.wait_ge(s["k_hi"], 4 * p)
                d.tensor_tensor(tmp[:, 1, :], psum[:, 1, :], rinv[:, :], ALU.mult).then_inc(s["pr_evac"], 1)

            def k_lo(p):
                for hh in range(2):
                    dve.wait_ge(s["k_hi"], 4 * p + (hh + 1))
                    d.tensor_tensor(k_b[own[hh], hh, :], tmp[own[hh], 1, :], ka[own[hh], hh, :].bitcast(F32),
                                    ALU.subtract).then_inc(s["k_ready"], 1)

            def v_evac(p):
                dve.wait_ge(unit[1], 2 * (N_ATT + p) + 4)
                if not (isinstance(p, int) and p == 0):
                    dve.wait_ge(s["vtr"], p)
                d.tensor_tensor(tmp[:, 2, :], psum[:, 2, :], rinv[:, :], ALU.mult).then_inc(s["pr_evac"], 1)

            dve.wait_ge(s["f_done"], 1)
            d.tensor_tensor(fwork[:, FZ, :], psum[:, 3, :], rinv[:, :], ALU.mult).then_inc(s["f_z"], 1)
            dve.wait_ge(s["f_z"], 1)
            dve.wait_ge(s["wf_loaded"], 16 * (P // HEADS + 1))
            d.tensor_scalar(fwork[:, FB, :], fwork[:, FZ, :], bf[:, 0:1], 0.0, ALU.add,
                            ALU.min).then_inc(s["f_b"], 1)
            q_evac(0)
            k_evac(0)
            split_lo(N_ATT + 1, 0)
            dve.wait_ge(s["f_b"], 1)
            dve.wait_ge(s["f_ln"], 1)
            d.tensor_tensor(fwork[:, FLOG, :], fwork[:, FB, :], fwork[:, FLN, :],
                            ALU.subtract).then_inc(s["f_log"], 1)
            dve.wait_ge(s["f_log"], 1)
            dve.wait_ge(s["f_one"], 1)
            d.tensor_tensor_scan(fwork[:, FCUM, :], fwork[:, FONE, :], fwork[:, FLOG, :], 0.0,
                                 ALU.mult, ALU.add).then_inc(s["f_cum"], 1)
            dve.wait_ge(s["f_hi"], 1)
            dve.wait_ge(s["f_base"], 2)
            dve.wait_ge(s["sel_part"], 9)
            Fh = Fhi[:, :].bitcast(F32)
            d.tensor_tensor(fwork[:, FZ, :], fwork[:, FCUM, :], Fh, ALU.subtract).then_inc(s["f_lo"], 1)
            q_lo(0)
            dve.wait_ge(s["f_lo"], 1)
            dve.wait_ge(s["f_part"], 2)
            d.scalar_tensor_tensor(gates_q[:, :], fwork[:, FZ, :], part[:, MINUS_QLO:MINUS_QLO + 1],
                                   fwork[:, FEXP, :], ALU.mult, ALU.add).then_inc(s["f_rows"], 1)
            for hh in range(2):
                rows = other[hh]
                d.scalar_tensor_tensor(k_b[rows, hh, :], fwork[rows, FZ, :], part[rows, KLO:KLO + 1],
                                       fwork[rows, FABS, :], ALU.mult, ALU.add).then_inc(s["f_rows"], 1)
            k_lo(0)
            v_evac(0)
            split_lo(N_ATT + 1, 1)

            def attention(p, project):
                def normalise(i):
                    hh, j = i // 4, i % 4
                    dve.wait_ge(s["ex_done"], 8 * p + (i + 1))
                    d.reciprocal(rden[:, i:i + 1], den[:, i:i + 1]).then_inc(s["rc_done"], 1)
                    dve.wait_ge(s["rc_done"], 8 * p + (i + 1))
                    pr = probs(hh, j)
                    d.tensor_scalar(pr, pr, rden[:, i:i + 1], None, ALU.mult).then_inc(s["p_ready"], 1)

                for what, i in SEQ:
                    hh, j = i // 4, i % 4
                    if what == "S":
                        dve.wait_ge(s["sc_done"], 8 * p + (i + 1))
                        dve.wait_ge(s["t_done"], 8 * p + (i + 1))
                        d.sem_inc(s["sc_seen"], 1)
                        d.tensor_tensor_reduce(out=probs(hh, j), in0=psum[:, SCORE + i % 2, 0:(j + 1) * P],
                                               in1=causal[:, S - (j + 1) * P:S], scale=1.0, scalar=3e38,
                                               op0=ALU.add, op1=ALU.min,
                                               accum_out=negmax[:, i:i + 1]).then_inc(s["sc_evac"], 1)
                        if i >= 1:
                            normalise(i - 1)
                        if i == 7:
                            normalise(7)
                    if what == "V":
                        dve.wait_ge(s["v_hi"], p + 1)
                        d.tensor_tensor(flat(vlo[:, :, :]), psum[:, 3, :], flat(vhi[:, :, :]).bitcast(F32),
                                        ALU.subtract).then_inc(s["v_ready"], 1)
                    if what == "EVAC" and project:
                        (q_evac, k_evac, v_evac)[i](p + 1)
                    if what == "PARTS" and project:
                        (q_lo, k_lo)[i](p + 1)
                    if what == "SPLIT" and project:
                        if i < 2:
                            split_lo(N_ATT + 2 + p, i)
                        else:
                            split_lo(N_ATT + 1 + p, 2, single=True)
                    if what == "SPLIT" and not project and i == 2:
                        split_lo(N_WO, 2)
                        split_lo(N_WO, 3)
                    if what == "T":
                        dve.wait_ge(s["p_hi"], 8 * p + (i + 1))
                        src = psum[:, TRP[i % 2], 0:(j + 1) * P].rearrange("p (a b) -> p a b", b=P)
                        d.tensor_tensor(pTlo[:, 0:j + 1, j * P:(j + 1) * P], src,
                                        pThi[:, 0:j + 1, j * P:(j + 1) * P].bitcast(F32),
                                        ALU.subtract).then_inc(s["pt_ready"], 1)
                    if what == "O":
                        dve.wait_ge(s["o_hi"], 2 * p + (i + 1))
                        rows = slice(HD * i, HD * i + HD)
                        if isinstance(p, int):
                            dst, hi = olo[rows, p, :], ohi[rows, p, :]
                        else:
                            dst, hi = flat(olo[rows, ds(p, 1), :]), flat(ohi[rows, ds(p, 1), :])
                        d.tensor_tensor(dst, psum[rows, OUTP, :], hi.bitcast(F32),
                                        ALU.subtract).then_inc(s["o_ready"], 1)

            with dve.Fori(0, PAIRS - 2) as p:
                attention(p, True)
            attention(PAIRS - 2, True)
            attention(PAIRS - 1, False)
            mixer_out(N_WO, 2)
            boundary(2, V_MIX_POST + 1, 3, V_FFN_PRE + 1, N_MLP1 + 1)
            mlp(1, N_MLP1, 3, True)
            boundary(3, V_FFN_POST + 1, None, None)


_INS = ["x", "g_mix_pre", "g_mix_post", "g_ffn_pre", "g_ffn_post", "conv_pw1_w", "conv_pw1_b",
        "conv_dw_w", "conv_dw_b", "conv_ln_g", "conv_ln_b", "conv_pw2_w", "conv_pw2_b", "attn_w_in",
        "attn_b_f", "attn_w_o", "mlp_w_up", "mlp_w_down"]


def kernel(**inputs):
    import numpy as np
    import concourse.bacc as bacc
    from concourse import mybir as mb
    from concourse.bass_utils import run_bass_kernel_spmd as run

    nc = bacc.Bacc("TRN2", target_bir_lowering=False, num_devices=1)
    arrays, args = {}, []
    for name in _INS:
        a = np.ascontiguousarray(inputs[name])
        arrays[f"in_{name}"] = a
        args.append(nc.dram_tensor(f"in_{name}", a.shape, mb.dt.from_np(a.dtype),
                                   kind="ExternalInput").ap())
    args.append(nc.dram_tensor("out_x", (1, S, D), F32, kind="ExternalOutput").ap())
    build(nc, *args)
    r = run(nc, [arrays], core_ids=[0])
    return r.results[0]["out_x"]
```
